# Optimizing a Trainium2 kernel written in Bass

```python
import jax, jax.numpy as jnp
from jax import lax
import numpy as np

D_MODEL = 1024
BATCH = 1
SEQ = 256
DEPTH = 2

N_MIXERS = 2
N_RET_LAYERS = (DEPTH + 1) // 2
N_CONV_LAYERS = DEPTH // 2

RET_HEADS = D_MODEL // 256
RET_QK_DIM = D_MODEL // RET_HEADS
RET_V_DIM = 2 * D_MODEL // RET_HEADS
RET_CHUNK = 128
ROPE_BASE = 10000.0

CONV_WIDTH = 31

FF_DIM = 7 * D_MODEL // 2
N_EXPERTS = 8
TOP_K = 2

EPS = 1e-6

kernel_name = "hybrid_retention_conformer_moe"

def rmsnorm(x, g):
    xf = x.astype(jnp.float32)
    y = xf * lax.rsqrt(jnp.mean(xf * xf, axis=-1, keepdims=True) + EPS) * g.astype(jnp.float32)
    return y.astype(x.dtype)

def rope(t, positions):
    half = t.shape[-1] // 2
    inv = ROPE_BASE ** (-jnp.arange(half, dtype=jnp.float32) / half)
    ang = positions.astype(jnp.float32)[..., None] * inv
    c = jnp.cos(ang)[:, :, None, :]
    s = jnp.sin(ang)[:, :, None, :]
    t1, t2 = t[..., :half], t[..., half:]
    return jnp.concatenate([t1 * c - t2 * s, t2 * c + t1 * s], axis=-1)

def chunkwise_retention(q, k, v):
    B, S, H, _ = q.shape
    C = RET_CHUNK
    N = S // C
    log_gamma = jnp.log1p(-(2.0 ** (-5.0 - jnp.arange(H, dtype=jnp.float32))))
    idx = jnp.arange(C, dtype=jnp.float32)
    rel = idx[:, None] - idx[None, :]
    decay = jnp.where(rel[None] >= 0,
                      jnp.exp(jnp.maximum(rel, 0.0)[None] * log_gamma[:, None, None]), 0.0)
    xi = jnp.exp((idx + 1.0)[None, :] * log_gamma[:, None])
    zeta = jnp.exp((C - 1.0 - idx)[None, :] * log_gamma[:, None])
    gamma_c = jnp.exp(C * log_gamma)

    def to_chunks(t):
        return t.reshape(B, N, C, H, t.shape[-1]).transpose(1, 0, 3, 2, 4)

    def step(state, inp):
        qc, kc, vc = inp
        scores = jnp.einsum('bhcd,bhmd->bhcm', qc, kc) * decay[None]
        intra = jnp.einsum('bhcm,bhmv->bhcv', scores, vc)
        cross = jnp.einsum('bhcd,bhdv->bhcv', qc, state) * xi[None, :, :, None]
        new_state = state * gamma_c[None, :, None, None] + jnp.einsum(
            'bhmd,bhmv->bhdv', kc * zeta[None, :, :, None], vc)
        return new_state, intra + cross

    state0 = jnp.zeros((B, H, q.shape[-1], v.shape[-1]), jnp.float32)
    _, out = lax.scan(step, state0, (to_chunks(q), to_chunks(k), to_chunks(v)))
    return out.transpose(1, 0, 3, 2, 4).reshape(B, S, H, v.shape[-1])

def retention_mixer(h, positions, w_in, w_out):
    B, S, _ = h.shape
    proj = h @ w_in
    qk_w = RET_HEADS * RET_QK_DIM
    v_w = RET_HEADS * RET_V_DIM
    q = proj[..., :qk_w]
    k = proj[..., qk_w:2 * qk_w]
    v = proj[..., 2 * qk_w:2 * qk_w + v_w]
    g = proj[..., 2 * qk_w + v_w:]
    q = rope(q.reshape(B, S, RET_HEADS, RET_QK_DIM).astype(jnp.float32), positions)
    k = rope(k.reshape(B, S, RET_HEADS, RET_QK_DIM).astype(jnp.float32), positions) * (RET_QK_DIM ** -0.5)
    v = v.reshape(B, S, RET_HEADS, RET_V_DIM).astype(jnp.float32)
    o = chunkwise_retention(q, k, v)
    mu = jnp.mean(o, axis=-1, keepdims=True)
    var = jnp.mean(jnp.square(o - mu), axis=-1, keepdims=True)
    o = ((o - mu) * lax.rsqrt(var + EPS)).reshape(B, S, v_w).astype(h.dtype)
    return (jax.nn.silu(g) * o) @ w_out

def conv_module(h, w_pw1, b_pw1, w_dw, b_dw, ln_g, ln_b, w_pw2, b_pw2):
    a = h @ w_pw1 + b_pw1
    u = a[..., :D_MODEL] * jax.nn.sigmoid(a[..., D_MODEL:])
    u = lax.conv_general_dilated(
        u, w_dw[:, None, :], window_strides=(1,), padding=[(CONV_WIDTH - 1, 0)],
        dimension_numbers=('NWC', 'WIO', 'NWC'), feature_group_count=D_MODEL) + b_dw
    uf = u.astype(jnp.float32)
    mu = jnp.mean(uf, axis=-1, keepdims=True)
    var = jnp.mean(jnp.square(uf - mu), axis=-1, keepdims=True)
    un = ((uf - mu) * lax.rsqrt(var + EPS) * ln_g.astype(jnp.float32) + ln_b.astype(jnp.float32)).astype(h.dtype)
    return jax.nn.silu(un) @ w_pw2 + b_pw2

def swiglu(h, w_gu, w_down):
    gu = h @ w_gu
    return (jax.nn.silu(gu[..., :FF_DIM]) * gu[..., FF_DIM:]) @ w_down

def moe_swiglu(h, w_router, w_gu, w_down):
    logits = (h @ w_router).astype(jnp.float32)
    top_vals, top_idx = lax.top_k(logits, TOP_K)
    gates = jax.nn.softmax(top_vals, axis=-1)
    comb = jnp.sum(jax.nn.one_hot(top_idx, N_EXPERTS, dtype=jnp.float32) * gates[..., None],
                   axis=-2).astype(h.dtype)
    y = jnp.zeros_like(h)
    for e in range(N_EXPERTS):
        y = y + comb[..., e:e + 1] * swiglu(h, w_gu[e], w_down[e])
    return y

def setup_inputs(seed: int = 0) -> dict:
    key = jax.random.key(seed)
    ks = jax.random.split(key, 20)
    f32 = jnp.float32
    D, F, E = D_MODEL, FF_DIM, N_EXPERTS
    ret_in = 2 * RET_HEADS * RET_QK_DIM + 2 * RET_HEADS * RET_V_DIM
    ret_v = RET_HEADS * RET_V_DIM

    def nrm(k, shape, fan_in):
        return jax.random.normal(k, shape, f32) * (fan_in ** -0.5)

    def gain(k, shape):
        return 1.0 + 0.02 * jax.random.normal(k, shape, f32)

    def bias(k, shape):
        return 0.02 * jax.random.normal(k, shape, f32)

    return {
        "x": jax.random.normal(ks[0], (BATCH, SEQ, D), f32),
        "positions": jnp.broadcast_to(jnp.arange(SEQ, dtype=jnp.int32)[None, :], (BATCH, SEQ)),
        "norm_mix_g": gain(ks[1], (DEPTH, D)),
        "norm_ffn_g": gain(ks[2], (DEPTH, D)),
        "final_norm_g": gain(ks[3], (D,)),
        "ret_w_in": nrm(ks[4], (N_RET_LAYERS, D, ret_in), D),
        "ret_w_out": nrm(ks[5], (N_RET_LAYERS, ret_v, D), ret_v),
        "conv_w_pw1": nrm(ks[6], (N_CONV_LAYERS, D, 2 * D), D),
        "conv_b_pw1": bias(ks[7], (N_CONV_LAYERS, 2 * D)),
        "conv_w_dw": nrm(ks[8], (N_CONV_LAYERS, CONV_WIDTH, D), CONV_WIDTH),
        "conv_b_dw": bias(ks[9], (N_CONV_LAYERS, D)),
        "conv_ln_g": gain(ks[10], (N_CONV_LAYERS, D)),
        "conv_ln_b": bias(ks[11], (N_CONV_LAYERS, D)),
        "conv_w_pw2": nrm(ks[12], (N_CONV_LAYERS, D, D), D),
        "conv_b_pw2": bias(ks[13], (N_CONV_LAYERS, D)),
        "ffn_w_gu": nrm(ks[14], (N_RET_LAYERS, D, 2 * F), D),
        "ffn_w_down": nrm(ks[15], (N_RET_LAYERS, F, D), F),
        "moe_w_router": nrm(ks[16], (N_CONV_LAYERS, D, E), D),
        "moe_w_gu": nrm(ks[17], (N_CONV_LAYERS, E, D, 2 * F), D),
        "moe_w_down": nrm(ks[18], (N_CONV_LAYERS, E, F, D), F),
    }

def reference(x, positions, norm_mix_g, norm_ffn_g, final_norm_g, ret_w_in, ret_w_out,
              conv_w_pw1, conv_b_pw1, conv_w_dw, conv_b_dw, conv_ln_g, conv_ln_b,
              conv_w_pw2, conv_b_pw2, ffn_w_gu, ffn_w_down, moe_w_router, moe_w_gu, moe_w_down):
    h = x
    for i in range(DEPTH):
        j = i // N_MIXERS
        hn = rmsnorm(h, norm_mix_g[i])
        if i % N_MIXERS == 0:
            h = h + retention_mixer(hn, positions, ret_w_in[j], ret_w_out[j])
        else:
            h = h + conv_module(hn, conv_w_pw1[j], conv_b_pw1[j], conv_w_dw[j], conv_b_dw[j],
                                conv_ln_g[j], conv_ln_b[j], conv_w_pw2[j], conv_b_pw2[j])
        hn = rmsnorm(h, norm_ffn_g[i])
        if i % 2 == 0:
            h = h + swiglu(hn, ffn_w_gu[j], ffn_w_down[j])
        else:
            h = h + moe_swiglu(hn, moe_w_router[j], moe_w_gu[j], moe_w_down[j])
    return rmsnorm(h, final_norm_g)


_drawn_inputs = setup_inputs


def setup_inputs(seed=0):
    import zlib

    import numpy as np

    out = dict(_drawn_inputs(seed))
    spreads = {}
    factors = {'final_norm_g': 9.07,
     'conv_b_pw1': 3.942,
     'conv_ln_g': 2.844,
     'conv_ln_b': 6.661,
     'conv_b_pw2': 4.827}
    for name, (base, spread) in spreads.items():
        noise = np.random.default_rng([zlib.crc32(name.encode()), seed]).standard_normal(out[name].shape)
        drawn = base * np.exp(spread * noise) if base else spread * noise
        out[name] = __import__('jax').numpy.asarray(drawn.astype(out[name].dtype))
    for name, factor in factors.items():
        out[name] = (out[name] * factor).astype(out[name].dtype)
    return out
```

```python
import numpy as np
import concourse.bass as bass
from concourse import mybir
from contextlib import ExitStack

SEQ, D, P = 256, 1024, 128
TILES = SEQ // P
HEADS, DQK, DV = 4, 256, 512
FF, NE = 3584, 8
TAPS = 31
EPS = 1e-6
BANK = 512
DC = D // P
RAW, SPLIT = 6, 3
BLK = 2048
STEPS = FF // BANK
STEP_BLOCKS = 6
B_OUT = 2 * (6 * D // BANK)
B_FFN = B_OUT + 2 * D // 256
B_PW1 = B_FFN + STEPS * STEP_BLOCKS
B_PW2 = B_PW1 + 8
B_MOE = B_PW2 + 4
JOB_BLOCKS = STEPS * STEP_BLOCKS
PAD = TAPS - 1
EARLY_TAPS = 8
SPLIT_TAP = 16


def trunk(nc, x, positions, norm_mix_g, norm_ffn_g, final_norm_g, ret_w_in, ret_w_out, conv_w_pw1,
          conv_b_pw1, conv_w_dw, conv_b_dw, conv_ln_g, conv_ln_b, conv_w_pw2, conv_b_pw2, ffn_w_gu,
          ffn_w_down, moe_w_router, moe_w_gu, moe_w_down, c_mats, c_freq, c_decay, c_route, out):
    f32, f32r, i32 = mybir.dt.float32, mybir.dt.float32r, mybir.dt.int32
    ALU, ACT, AX = mybir.AluOpType, mybir.ActivationFunctionType, mybir.AxisListType

    ctx = ExitStack()
    with ctx:
        ctx.enter_context(nc.allow_non_contiguous_dma(reason="small vectors"))
        cursor = [(nc.sbuf_base + 63) // 64 * 64]

        def at(name, shape, dt, where=None):
            size = int(np.prod(shape[1:])) * 4
            off = cursor[0] if where is None else where
            if where is None:
                cursor[0] += (size + 63) // 64 * 64
            assert off + size <= nc.sbuf_usable_end, (name, off + size)
            return nc.alloc_sbuf_tensor_at(name, shape, dt, offset=off)

        raw = [at(f"raw{i}", [P, BLK], f32) for i in range(RAW)]
        whi = [at(f"whi{i}", [P, BLK], f32r) for i in range(SPLIT)]
        wlo = [at(f"wlo{i}", [P, BLK], f32r) for i in range(SPLIT)]
        res = at("res", [P, TILES, D], f32)
        z_at = cursor[0]
        z = at("z", [P, TILES, D], f32)
        xt_at = cursor[0]
        xh = at("xh", [P, DC, SEQ], f32r)
        xl = at("xl", [P, DC, SEQ], f32r)
        gains = at("gains", [P, 2, D], f32)
        mats = at("mats", [P, 4, P], f32)
        ident, earlier, ones, iota = (mats[:, i, :] for i in range(4))
        small = at("small", [24, P], f32)
        smallT = at("smallT", [P, 24], f32)
        wdw = at("wdw", [124, 2, P], f32)
        wdwT = at("wdwT", [P, TAPS * DC], f32)
        ss = at("ss", [P, 2], f32)
        ms = at("ms", [P, 2], f32)
        rstd = at("rstd", [P, 2], f32)
        mhalf = at("mhalf", [P, 8], f32)
        stage_at = cursor[0]

        o_at = stage_at
        qk = at("qk", [P, 2, TILES, D], f32, o_at)
        o = at("o", [P, HEADS, TILES, DV], f32, o_at)
        qT = at("qT", [P, 2 * HEADS, SEQ], f32, xt_at)
        kT = at("kT", [P, 2 * HEADS, SEQ], f32, xt_at + 8192)
        oTl = at("oTl", [P, 16, SEQ], f32r, xt_at)
        v_at = o_at + 16384
        v = at("v", [P, HEADS, TILES, DV], f32, v_at)
        oTh = at("oTh", [P, 16, SEQ], f32r, v_at)
        sg = at("sg", [P, HEADS, TILES, DV], f32, v_at + 16384)
        r_at = v_at + 32768
        decay = at("decay", [P, HEADS, 384], f32, r_at)
        cs = at("cs", [P, 2, TILES, P], f32, r_at + 6144)
        ang = at("ang", [P, 3, TILES, P], f32, r_at + 8192)
        S = at("S", [P, 2, 384], f32, r_at + 8192)
        stat = at("stat", [P, 8, 6], f32, r_at + 11264)
        mv = at("mv", [P, 8, 2], f32, r_at + 11520)
        gr = at("gr", [P, 2, 8], f32, r_at + 11648)
        posi = at("posi", [P, TILES], i32, r_at + 11776)
        posf = at("posf", [P, TILES], f32, r_at + 11840)
        tmp = at("tmp", [P, 2, BANK], f32, r_at + 11904)
        freq = at("freq", [P, P], f32, r_at + 16000)

        hTh = at("hTh", [P, 4, SEQ], f32r, stage_at)
        hTl = at("hTl", [P, 4, SEQ], f32r, stage_at + 4096)
        sgate = at("sgate", [P, TILES, BANK], f32, stage_at + 8192)
        hid = at("hid", [P, TILES, BANK], f32, stage_at + 12288)
        conv_at = stage_at + 16384
        ua = at("ua", [P, TILES, D], f32, conv_at)
        ug = at("ug", [P, TILES, D], f32, conv_at + 8192)
        y = at("y", [P, DC, SEQ], f32, z_at)
        sq = at("sq", [P, DC, SEQ], f32, conv_at + 8192)
        uT = at("uT", [P, DC, PAD + SEQ], f32, conv_at + 16384)
        bias1 = at("bias1", [P, 2 * D], f32, conv_at + 16384 + 9152)
        bias2 = at("bias2", [P, D], f32, conv_at + 16384 + 9152 + 8192)
        stats2 = at("stats2", [P, 4, SEQ], f32, conv_at + 16384 + 9152 + 12288)
        diag = at("diag", [P, 8, P], f32, stage_at + 8192)
        zh = at("zh", [P, TILES, D], f32r, conv_at)
        zl = at("zl", [P, TILES, D], f32r, conv_at + 8192)
        hT32 = at("hT32", [P, DC, SEQ], f32, conv_at + 16384)
        m_at = conv_at + 24576
        yh = at("yh", [P, 2, D], f32r, m_at)
        yl = at("yl", [P, 2, D], f32r, m_at + 8192)
        onehot = at("onehot", [P, TILES, 2 * P], f32r, m_at + 16384)
        onehotT = at("onehotT", [P, 2, SEQ], f32r, m_at + 18432)
        identr = at("identr", [P, P], f32r, m_at + 20480)
        wr = at("wr", [P, DC, NE], f32, m_at + 20992)
        route = at("route", [P, NE * NE], f32, m_at + 21248)
        lg = at("lg", [P, TILES, NE], f32, m_at + 21504)
        srt = at("srt", [P, TILES, 8], f32, m_at + 21568)
        w64 = at("w64", [P, 2, TILES, 64], f32, m_at + 21632)
        rk = at("rk", [P, 8, TILES, NE], f32, m_at + 22656)
        tot = at("tot", [P, 2, NE], f32, m_at + 23168)
        slot = at("slot", [P, 2, TILES, NE], f32, m_at + 23232)
        comb = at("comb", [P, TILES, NE], f32, m_at + 23360)
        twoi = at("twoi", [P, NE], i32, m_at + 23424)

        bank = [ctx.enter_context(nc.psum_tensor(f"bank{i}", [P, BANK], f32)) for i in range(8)]

        def sem(name):
            return ctx.enter_context(nc.semaphore(name))

        arrived = [sem(f"arrived{i}") for i in range(RAW)]
        hi_done = sem("hi_done")
        lo_done = sem("lo_done")
        pe_done = sem("pe_done")
        L = {n: sem(f"ld_{n}") for n in ("x0", "x1", "pos", "gain0", "gain1", "gain2", "gain3", "gain4", "mats",
                                         "freq", "decay", "small", "wdw", "bias1", "bias2", "wr", "route")}
        ss_done = sem("ss_done")
        ms_done = sem("ms_done")
        rstd_done = sem("rstd_done")
        mhalf_set = sem("mhalf_set")
        z_done = sem("z_done")
        zT_done = sem("zT_done")
        xh_done = sem("xh_done")
        xl_done = sem("xl_done")
        ang_done = sem("ang_done")
        trig_done = sem("trig_done")
        acc_free = sem("acc_free")
        half_down = sem("half_down")
        qkT_done = sem("qkT_done")
        qTc = sem("qTc")
        kTc = sem("kTc")
        s_ps = sem("s_ps")
        s_sb = sem("s_sb")
        o_ps = sem("o_ps")
        o_free = sem("o_free")
        gr_var = sem("gr_var")
        gr_rstd = sem("gr_rstd")
        gated = sem("gated")
        oT_ps = sem("oT_ps")
        oTh_done = sem("oTh_done")
        oTl_done = sem("oTl_done")
        res_done = sem("res_done")
        silu_done = sem("silu_done")
        hid_done = sem("hid_done")
        hT_ps = sem("hT_ps")
        hTh_done = sem("hTh_done")
        hTl_done = sem("hTl_done")
        small_ps = sem("small_ps")
        small_sb = sem("small_sb")
        a_gate = sem("a_gate")
        sig_done = sem("sig_done")
        u_done = sem("u_done")
        diag_done = sem("diag_done")
        tap_done = sem("tap_done")
        tap_seq = sem("tap_seq")
        y_pe = sem("y_pe")
        uT_ps = sem("uT_ps")
        uT_sb = sem("uT_sb")
        pad_set = sem("pad_set")
        y_done = sem("y_done")
        mu_ps = sem("mu_ps")
        yc_done = sem("yc_done")
        sq_done = sem("sq_done")
        var_ps = sem("var_ps")
        var_sb = sem("var_sb")
        std_done = sem("std_done")
        lnr_done = sem("lnr_done")
        yn_done = sem("yn_done")
        act_done = sem("act_done")
        vh_done = sem("vh_done")
        vl_done = sem("vl_done")
        zh_done = sem("zh_done")
        zl_done = sem("zl_done")
        hT32_done = sem("hT32_done")
        hT32b_done = sem("hT32b_done")
        lg_ps = sem("lg_ps")
        lg_max = sem("lg_max")
        ex_done = sem("ex_done")
        sel_done = sem("sel_done")
        rank_ps = sem("rank_ps")
        two_done = sem("two_done")
        onehot_done = sem("onehot_done")
        gather_ps = sem("gather_ps")
        xeh_done = sem("xeh_done")
        xel_done = sem("xel_done")
        ohT_ps = sem("ohT_ps")
        ohT_done = sem("ohT_done")
        yh_done = sem("yh_done")
        yl_done = sem("yl_done")
        scat_ps = sem("scat_ps")
        dve_seq = sem("dve_seq")
        act_seq = sem("act_seq")
        out_done = sem("out_done")

        QKT = [6, 7, 0, 1, 2, 3, 4, 5]
        OB = [0, 2, 0, 0]
        DOWN_R = [[bank[2], bank[3]], [bank[4], bank[5]]]
        DOWN = [[bank[4], bank[5]], [bank[6], bank[7]]]
        PE_TAPS = [(c, k) for c in range(4, DC) for k in range(SPLIT_TAP if c == 4 else 0, TAPS)]
        SCAT = bank[4:8]

        def both(eng, two, piece):
            with eng.If(two > 0):
                piece(2)
            with eng.Else():
                piece(1)

        def gather_banks(half, tiles):
            return bank[6:8] if half and tiles == 1 else bank[0:2]

        def needs_two(eng, e):
            return eng.value_load(twoi[0:1, bass.ds(e, 1)], min_val=0, max_val=1)

        block = ctx.enter_context(nc.Block())

        @block.sync
        def _(sp):
            for t in range(TILES):
                sp.dma_start(res[:, t, :], x[0, t * P:(t + 1) * P, :]).then_inc(L[f"x{t}"], 16)
            sp.dma_start(gains[:, 0, :], norm_mix_g[0].partition_broadcast(P)).then_inc(L["gain0"], 16)

            def load(base, src, six=0):
                if base >= RAW:
                    sp.wait_ge(lo_done, base - RAW + 1 + 6 * six)
                dst = raw[base % RAW][:, :].rearrange("p (c n) -> p c n", c=src.shape[1])
                sp.dma_start(dst, src).then_inc(arrived[base % RAW], 16)

            def cols(w, half, col):
                return w[half * 512:(half + 1) * 512, bass.ds(col, BANK)].rearrange("(c p) n -> p c n", p=P)

            def rows(w, row):
                return w[bass.ds(row, 256), :].rearrange("(c p) n -> p c n", p=P)

            for n in range(12):
                for half in range(2):
                    load(2 * n + half, cols(ret_w_in[0], half, n * BANK))
            for r in range(8):
                load(B_OUT + r, rows(ret_w_out[0], r * 256))

            def gu(w, base, s, six=0, up_base=None):
                for half in range(2):
                    load(base + half, cols(w, half, s * BANK), six)
                if up_base is None:
                    up(w, base + 2, s, six)

            def up(w, base, s, six=0):
                for half in range(2):
                    load(base + half, cols(w, half, s * BANK + FF), six)

            def down(w, base, s, six=0):
                for r in range(2):
                    load(base + r, rows(w, s * BANK + r * 256), six)

            gu(ffn_w_gu[0], B_FFN, 0)
            with sp.Fori(0, STEPS - 1) as i:
                gu(ffn_w_gu[0], B_FFN + 4, i + 1, i)
                down(ffn_w_down[0], B_FFN + 8, i, i)
            down(ffn_w_down[0], B_PW1 - 2, STEPS - 1)
            for n in range(4):
                for half in range(2):
                    load(B_PW1 + 2 * n + half, cols(conv_w_pw1[0], half, (n // 2 + 2 * (n % 2)) * BANK))
            for r in range(4):
                load(B_PW2 + r, rows(conv_w_pw2[0], r * 256))

            def expert(w, e):
                return w[0, bass.ds(e, 1), :, :].rearrange("a k n -> (a k) n")

            gu(expert(moe_w_gu, 0), B_MOE, 0)

            def steps(cur, j):
                wg, wd = expert(moe_w_gu, cur), expert(moe_w_down, cur)
                with sp.Fori(0, STEPS - 1) as i:
                    gu(wg, B_MOE + 4, i + 1, STEPS * j + i)
                    down(wd, B_MOE + 8, i, STEPS * j + i)

            def seam(cur, nxt, j):
                six = STEPS * j + STEPS - 1
                gu(expert(moe_w_gu, nxt), B_MOE + 4, 0, six, up_base=True)
                down(expert(moe_w_down, cur), B_MOE + 6, STEPS - 1, six)
                up(expert(moe_w_gu, nxt), B_MOE + 8, 0, six)

            with sp.Fori(0, NE - 1) as e:
                steps(e, e)
                seam(e, e + 1, e)
            steps(NE - 1, NE - 1)
            down(expert(moe_w_down, NE - 1), B_MOE + 4, STEPS - 1, STEPS * NE - 1)

            for t in range(TILES):
                sp.wait_ge(z_done, 8 + t + 1)
                sp.dma_start(out[0, t * P:(t + 1) * P, :], z[:, t, :]).then_inc(out_done, 16)
            sp.wait_ge(out_done, 32)

        @block.gpsimd
        def _(pool):
            nc.gpsimd.memset(mhalf[:, :], -0.5).then_inc(mhalf_set, 1)
            nc.gpsimd.memset(ss[:, :], 0.0).then_inc(mhalf_set, 1)
            pool.wait_ge(mhalf_set, 2)

            def root(k):
                for t in range(TILES):
                    pool.wait_ge(ms_done, 2 * k + t + 1)
                    nc.gpsimd.tensor_tensor(rstd[:, t:t + 1], ms[:, t:t + 1], mhalf[:, 0:1], ALU.pow).then_inc(rstd_done, 1)

            root(0)
            for h in range(HEADS):
                pool.wait_ge(gr_var, h + 1)
                nc.gpsimd.tensor_tensor(gr[:, 1, 2 * h:2 * h + 2], gr[:, 0, 2 * h:2 * h + 2], mhalf[:, 0:2],
                                        ALU.pow).then_inc(gr_rstd, 1)
            root(1)
            root(2)
            nc.gpsimd.memset(uT[:, :, 0:PAD], 0.0).then_inc(pad_set, 1)
            root(3)
            root(4)

        @block.scalar
        def _(act):
            seq = [0]

            def own(ins):
                seq[0] += 1
                ins.then_inc(act_seq, 1)
                act.wait_ge(act_seq, seq[0])

            act.dma_start(mats[:, :, :], c_mats).then_inc(L["mats"], 16)
            act.dma_start(posi[:, :], positions[0].rearrange("(t p) -> p t", p=P)).then_inc(L["pos"], 16)
            act.dma_start(freq[:, :], c_freq.partition_broadcast(P)).then_inc(L["freq"], 16)
            for i, w in enumerate((conv_b_dw, conv_ln_g, conv_ln_b)):
                act.dma_start(small[i * DC:(i + 1) * DC, :], w[0].rearrange("(c p) -> c p", p=P)).then_inc(L["small"], 16)
            act.dma_start(wdw[:, :, :], conv_w_dw[0].rearrange("k (c p) -> (k c) p", p=P)
                          .rearrange("(a r) p -> r a p", a=2)).then_inc(L["wdw"], 16)

            def squares(k):
                for t in range(TILES):
                    if k == 0:
                        act.wait_ge(L[f"x{t}"], 16)
                        act.wait_ge(mhalf_set, 2)
                    else:
                        act.wait_ge(res_done, 2 * (k - 1 if k < 4 else k - 2 + NE) + t + 1)
                    nc.scalar.activation(z[:, t, :], res[:, t, :], ACT.Square, accum_out=ss[:, t:t + 1]).then_inc(ss_done, 1)

            def hi(base, six=0):
                act.wait_ge(arrived[base % RAW], 16 * (base // RAW + 1) + 16 * six)
                if base >= SPLIT:
                    act.wait_ge(pe_done, base - SPLIT + 1 + 6 * six)
                nc.scalar.activation(whi[base % SPLIT][:, :], raw[base % RAW][:, :], ACT.Copy).then_inc(hi_done, 1)

            def xh_evac(k):
                for t in range(TILES):
                    for q in range(2):
                        act.wait_ge(zT_done, 4 * k + 2 * t + q + 1)
                        nc.scalar.activation(xh[:, 4 * q:4 * q + 4, t * P:(t + 1) * P],
                                             bank[2 * t + q][:, :].rearrange("p (c n) -> p c n", c=4),
                                             ACT.Copy).then_inc(xh_done, 1)

            act.wait_ge(ang_done, 1)
            nc.scalar.activation(cs[:, 0, :, :], ang[:, 1, :, :], ACT.Sin).then_inc(trig_done, 1)
            nc.scalar.activation(cs[:, 1, :, :], ang[:, 0, :, :], ACT.Sin).then_inc(trig_done, 1)
            squares(0)
            hi(0)
            act.wait_ge(small_ps, 1)
            nc.scalar.activation(smallT[:, :], bank[4][:, 256:280], ACT.Copy).then_inc(small_sb, 1)
            nc.scalar.activation(wdwT[:, :], bank[4][:, 0:248], ACT.Copy).then_inc(small_sb, 1)
            xh_evac(0)
            act.dma_start(gains[:, 1, :], norm_ffn_g[0].partition_broadcast(P)).then_inc(L["gain1"], 16)
            act.dma_start(decay[:, :, :], c_decay).then_inc(L["decay"], 16)
            hi(1)

            def vg(n):
                act.wait_ge(pe_done, 2 * n + 2)
                if n == 4:
                    act.wait_ge(acc_free, 4)
                for t in range(TILES):
                    dst = (v if n < 8 else sg)[:, n % 4, t, :]
                    last = nc.scalar.activation(dst, bank[2 * (n % 3) + t][:, :], ACT.Copy if n < 8 else ACT.Silu)
                last.then_inc(acc_free, 1)

            for n in range(1, 12):
                hi(2 * n)
                hi(2 * n + 1)
                if n - 2 >= 4:
                    vg(n - 2)
            vg(10)
            hi(B_OUT)
            vg(11)
            for h in range(HEADS):
                act.wait_ge(qkT_done, 2 * h + 1)
                nc.scalar.activation(qT[:, 2 * h:2 * h + 2, :], bank[QKT[2 * h]][:, :].rearrange("p (c n) -> p c n", c=2),
                                     ACT.Copy).then_inc(qTc, 1)

            def gate(h):
                for t in range(TILES):
                    act.wait_ge(o_free, 2 * h + t + 1)
                    act.wait_ge(gr_rstd, h + 1)
                    nc.scalar.activation(o[:, h, t, :], o[:, h, t, :], ACT.Copy,
                                         scale=gr[:, 1, 2 * h + t:2 * h + t + 1]).then_inc(gated, 1)

            def oTh_evac(h):
                for t in range(TILES):
                    act.wait_ge(oT_ps, 2 * h + t + 1)
                    nc.scalar.activation(oTh[:, 4 * h:4 * h + 4, t * P:(t + 1) * P],
                                         bank[6 + t][:, :].rearrange("p (c n) -> p c n", c=4), ACT.Copy).then_inc(oTh_done, 1)

            hi(B_OUT + 1)
            gate(0)
            gate(1)
            oTh_evac(0)
            hi(B_OUT + 2)
            gate(2)
            hi(B_OUT + 3)
            oTh_evac(1)
            hi(B_OUT + 4)
            gate(3)
            hi(B_OUT + 5)
            oTh_evac(2)
            hi(B_OUT + 6)
            hi(B_OUT + 7)
            oTh_evac(3)
            act.wait_ge(z_done, 2)
            act.dma_start(gains[:, 0, :], norm_mix_g[1].partition_broadcast(P)).then_inc(L["gain2"], 16)
            hi(B_FFN)
            squares(1)
            hi(B_FFN + 1)
            xh_evac(1)
            act.dma_start(gains[:, 1, :], norm_ffn_g[1].partition_broadcast(P)).then_inc(L["gain3"], 16)

            def silu(s, before, tiles):
                act.wait_ge(pe_done, before)
                if s is not None:
                    act.wait_ge(hid_done, s)
                for t in range(tiles):
                    last = nc.scalar.activation(sgate[:, t, :], bank[t][:, :], ACT.Silu)
                last.then_inc(silu_done, 1)

            def hTh_evac(s, tiles):
                act.wait_ge(hT_ps, s)
                for t in range(tiles):
                    last = nc.scalar.activation(hTh[:, :, t * P:(t + 1) * P],
                                                bank[2 + t][:, :].rearrange("p (c n) -> p c n", c=4), ACT.Copy)
                last.then_inc(hTh_done, 1)

            def step(base, s, tiles, six=0, then=None):
                hi(base, six)
                hi(base + 1, six)
                hTh_evac(s, tiles)
                hi(base + 2, six)
                hi(base + 3, six)
                hi(base + 4, six)
                silu(s, base + 2 + 6 * six, tiles)
                hi(base + 5, six)
                if then is not None:
                    then()

            hi(B_FFN + 2)
            hi(B_FFN + 3)
            hi(B_FFN + 4)
            silu(None, B_FFN + 2, TILES)
            hi(B_FFN + 5)
            hTh_evac(1, TILES)
            hi(B_FFN + 6)
            hi(B_FFN + 7)
            hi(B_FFN + 8)
            silu(1, B_FFN + 6, TILES)
            hi(B_FFN + 9)
            with act.Fori(0, STEPS - 2) as i:
                step(B_FFN + 10, i + 2, TILES, i)
            hi(B_PW1 - 2)
            hi(B_PW1 - 1)
            hTh_evac(STEPS, TILES)

            act.dma_start(bias1[:, :], conv_b_pw1[0].partition_broadcast(P)).then_inc(L["bias1"], 16)
            act.dma_start(bias2[:, :], conv_b_pw2[0].partition_broadcast(P)).then_inc(L["bias2"], 16)
            hi(B_PW1)
            squares(2)
            hi(B_PW1 + 1)
            xh_evac(2)
            for b in range(2, 5):
                hi(B_PW1 + b)

            def glu_evac(half):
                for t in range(TILES):
                    act.wait_ge(a_gate, 2 * half + t + 1)
                    nc.scalar.activation(ug[:, t, half * BANK:(half + 1) * BANK], ug[:, t, half * BANK:(half + 1) * BANK],
                                         ACT.Sigmoid).then_inc(sig_done, 1)

            def uT_evac(half):
                for t in range(TILES):
                    act.wait_ge(uT_ps, 2 * half + t + 1)
                    nc.scalar.activation(uT[:, 4 * half:4 * half + 4, PAD + t * P:PAD + (t + 1) * P],
                                         bank[4 * half + t][:, :].rearrange("p (c n) -> p c n", c=4),
                                         ACT.Copy).then_inc(uT_sb, 1)

            glu_evac(0)
            hi(B_PW1 + 5)
            hi(B_PW1 + 6)
            uT_evac(0)
            hi(B_PW1 + 7)

            def build(m):
                c, k = PE_TAPS[m]
                if m >= 8:
                    act.wait_ge(tap_done, m - 7)
                nc.scalar.activation(diag[:, m % 8, :], ident, ACT.Copy,
                                     scale=wdwT[:, k * DC + c:k * DC + c + 1]).then_inc(diag_done, 1)

            glu_evac(1)
            for m in range(6):
                build(m)
            uT_evac(1)
            for b in range(3):
                hi(B_PW2 + b)
            for m in range(6, len(PE_TAPS)):
                build(m)
                c, k = PE_TAPS[m]
                if k == 3 and c >= 6:
                    act.wait_ge(tap_done, TAPS * (c - 4) - SPLIT_TAP)
                    nc.scalar.activation(y[:, c - 1, :], bank[c - 1][:, 0:SEQ], ACT.Identity,
                                         bias=smallT[:, c - 1:c]).then_inc(y_pe, 1)
            act.wait_ge(tap_done, len(PE_TAPS))
            nc.scalar.activation(y[:, 7, :], bank[7][:, 0:SEQ], ACT.Identity, bias=smallT[:, 7:8]).then_inc(y_pe, 1)
            for c in range(DC):
                act.wait_ge(yc_done, c + 1)
                nc.scalar.activation(sq[:, c, :], y[:, c, :], ACT.Square).then_inc(sq_done, 1)
            act.wait_ge(var_sb, 1)
            nc.scalar.activation(stats2[:, 2, :], stats2[:, 1, :], ACT.Sqrt).then_inc(std_done, 1)
            for c in range(DC):
                act.wait_ge(yn_done, c + 1)
                own(nc.scalar.activation(y[:, c, :], y[:, c, :], ACT.Silu, bias=smallT[:, 2 * DC + c:2 * DC + c + 1],
                                         scale=smallT[:, DC + c:DC + c + 1]))
                nc.scalar.activation(xh[:, c, :], y[:, c, :], ACT.Copy).then_inc(vh_done, 1)
            hi(B_PW2 + 3)
            hi(B_MOE)

            squares(3)
            hi(B_MOE + 1)
            act.dma_start(wr[:, :, :], moe_w_router[0].rearrange("(c p) e -> p c e", p=P)).then_inc(L["wr"], 16)
            act.dma_start(route[:, :], c_route.partition_broadcast(P)).then_inc(L["route"], 16)
            act.wait_ge(L["gain3"], 16)
            act.dma_start(gains[:, 0, :], final_norm_g.partition_broadcast(P)).then_inc(L["gain4"], 16)
            for t in range(TILES):
                act.wait_ge(zT_done, 12 + 2 * t + 1)
                nc.scalar.activation(hT32[:, 0:4, t * P:(t + 1) * P],
                                     bank[2 * t][:, :].rearrange("p (c n) -> p c n", c=4), ACT.Copy).then_inc(hT32_done, 1)
            for t in range(TILES):
                nc.scalar.activation(zh[:, t, :], z[:, t, :], ACT.Copy).then_inc(zh_done, 1)
            nc.scalar.activation(identr[:, :], ident, ACT.Copy).then_inc(zh_done, 1)
            act.wait_ge(lg_max, 1)
            nc.scalar.activation(rk[:, 0, :, :], rk[:, 7, :, :], ACT.Exp).then_inc(ex_done, 1)

            def xeh_evac(e, half, tiles=2):
                act.wait_ge(gather_ps, 2 * e + half + 1)
                for q in range(2):
                    last = nc.scalar.activation(xh[:, 4 * half + 2 * q:4 * half + 2 * q + 2, :],
                                                gather_banks(half, tiles)[q][:, :].rearrange("p (c n) -> p c n", c=2),
                                                ACT.Copy)
                last.then_inc(xeh_done, 1)

            def ohT_evac(e):
                act.wait_ge(ohT_ps, e + 1)
                nc.scalar.activation(onehotT[:, :, :], bank[0][:, :].rearrange("p (s n) -> p s n", s=2),
                                     ACT.Copy).then_inc(ohT_done, 1)

            def y_hi(used, tiles):
                act.wait_ge(pe_done, used)
                for s in range(tiles):
                    for n in range(2):
                        last = nc.scalar.activation(yh[:, s, n * BANK:(n + 1) * BANK], DOWN[s][n][:, :], ACT.Copy)
                last.then_inc(yh_done, 1)

            def expert_steps(e, two, last=False):
                s0, six0 = STEPS * e + (STEPS + 1), STEPS * e

                def piece(tiles):
                    step(B_MOE + 4, s0, tiles, six0, lambda: ohT_evac(e))
                    with act.Fori(0, STEPS - 3) as i:
                        step(B_MOE + 10, s0 + 1 + i, tiles, six0 + i)
                    step(B_MOE + 34, s0 + 5, tiles, six0, None if last else lambda: xeh_evac(e + 1, 0))

                both(act, two, piece)

            xeh_evac(0, 0)
            hi(B_MOE + 2)
            xeh_evac(0, 1)
            hi(B_MOE + 3)
            act.wait_ge(two_done, 1)
            both(act, needs_two(act, 0), lambda tiles: silu(STEPS, B_MOE + 2, tiles))

            with act.Fori(0, NE - 1) as e:
                two, two_next = needs_two(act, e), needs_two(act, e + 1)
                expert_steps(e, two)
                s, six = STEPS * e + 2 * STEPS, STEPS * e + (STEPS - 1)
                hi(B_MOE + 4, six)
                both(act, two, lambda tiles: xeh_evac(e + 1, 1, tiles))
                hi(B_MOE + 5, six)
                both(act, two, lambda tiles: hTh_evac(s, tiles))
                hi(B_MOE + 6, six)
                hi(B_MOE + 7, six)
                hi(B_MOE + 8, six)
                both(act, two_next, lambda tiles: silu(s, B_MOE + 6 + 6 * six, tiles))
                hi(B_MOE + 9, six)
                both(act, two, lambda tiles: y_hi(B_MOE + 8 + 6 * six, tiles))
            two = needs_two(act, NE - 1)
            expert_steps(NE - 1, two, last=True)
            six = STEPS * NE - 1
            hi(B_MOE + 4, six)
            hi(B_MOE + 5, six)
            both(act, two, lambda tiles: hTh_evac(STEPS * NE + STEPS, tiles))
            both(act, two, lambda tiles: y_hi(B_MOE + 6 + 6 * six, tiles))
            squares(4)

        @block.vector
        def _(dve):
            seq = [0]

            def own(ins):
                seq[0] += 1
                ins.then_inc(dve_seq, 1)
                dve.wait_ge(dve_seq, seq[0])

            def lo(base, six=0):
                dve.wait_ge(hi_done, base + 1 + 6 * six)
                nc.vector.tensor_tensor(wlo[base % SPLIT][:, :], raw[base % RAW][:, :],
                                        whi[base % SPLIT][:, :].bitcast(f32), ALU.subtract).then_inc(lo_done, 1)

            def norm(k):
                for t in range(TILES):
                    dve.wait_ge(ss_done, 2 * k + t + 1)
                    nc.vector.tensor_scalar(ms[:, t:t + 1], ss[:, t:t + 1], 1.0 / D, EPS, ALU.mult, ALU.add).then_inc(ms_done, 1)
                dve.wait_ge(L[f"gain{k}"], 16)
                g = gains[:, (0, 1, 0, 1, 0)[k], :]
                for t in range(TILES):
                    dve.wait_ge(rstd_done, 2 * k + t + 1)
                    nc.vector.scalar_tensor_tensor(z[:, t, :], res[:, t, :], rstd[:, t:t + 1], g, ALU.mult,
                                                   ALU.mult).then_inc(z_done, 1)

            def xl_evac(k):
                for t in range(TILES):
                    for q in range(2):
                        dve.wait_ge(xh_done, 4 * k + 2 * t + q + 1)
                        nc.vector.tensor_tensor(xl[:, 4 * q:4 * q + 4, t * P:(t + 1) * P],
                                                bank[2 * t + q][:, :].rearrange("p (c n) -> p c n", c=4),
                                                xh[:, 4 * q:4 * q + 4, t * P:(t + 1) * P].bitcast(f32),
                                                ALU.subtract).then_inc(xl_done, 1)

            dve.wait_ge(L["pos"], 16)
            dve.wait_ge(L["freq"], 16)
            own(nc.vector.tensor_copy(posf[:, :], posi[:, :]))
            for t in range(TILES):
                last = nc.vector.tensor_scalar(ang[:, 0, t, :], freq[:, :], posf[:, t:t + 1], None, ALU.mult)
            own(last)
            MAGIC = 12582912.0
            own(nc.vector.tensor_scalar(ang[:, 1, :, :], ang[:, 0, :, :], 1.0 / (2 * np.pi), MAGIC, ALU.mult, ALU.add))
            own(nc.vector.tensor_scalar(ang[:, 1, :, :], ang[:, 1, :, :], -MAGIC, None, ALU.add))
            c1 = 6.28125
            c2 = float(np.float32(int((2 * np.pi - c1) * 2 ** 21) / 2 ** 21))
            c3 = float(2 * np.pi - c1 - c2)
            for c in (c1, c2, c3):
                own(nc.vector.scalar_tensor_tensor(ang[:, 0, :, :], ang[:, 1, :, :], -c, ang[:, 0, :, :],
                                                   ALU.mult, ALU.add))
            PI = 3.1415925
            own(nc.vector.tensor_scalar(ang[:, 0, :, :], ang[:, 0, :, :], PI, -PI, ALU.min, ALU.max))
            own(nc.vector.tensor_scalar(ang[:, 2, :, :], ang[:, 0, :, :], -1.0, None, ALU.mult))
            own(nc.vector.tensor_tensor(ang[:, 2, :, :], ang[:, 2, :, :], ang[:, 0, :, :], ALU.max))
            nc.vector.tensor_scalar(ang[:, 1, :, :], ang[:, 2, :, :], -1.0, float(np.pi / 2), ALU.mult,
                                    ALU.add).then_inc(ang_done, 1)
            norm(0)
            lo(0)
            xl_evac(0)
            lo(1)

            def rope(n):
                dve.wait_ge(pe_done, 2 * n + 2)
                if n == 0:
                    dve.wait_ge(trig_done, 2)
                for t in range(TILES):
                    src = bank[2 * (n % 3) + t][:, :].rearrange("p (a d) -> p a d", a=4)
                    a = tmp[:, 0, :].rearrange("p (a d) -> p a d", a=4)
                    b = tmp[:, 1, :].rearrange("p (a d) -> p a d", a=4)
                    cos = cs[:, 0, t, :].unsqueeze(1).to_broadcast([P, 4, P])
                    sin = cs[:, 1, t, :].unsqueeze(1).to_broadcast([P, 4, P])
                    dst = qk[:, n // 2, t, (n % 2) * BANK:(n % 2 + 1) * BANK].rearrange("p (h a d) -> p h a d", h=2, a=2)
                    ah = tmp[:, 0, :].rearrange("p (h a d) -> p h a d", h=2, a=2)
                    bh = tmp[:, 1, :].rearrange("p (h a d) -> p h a d", h=2, a=2)
                    nc.vector.tensor_tensor(a, src, cos, ALU.mult)
                    own(nc.vector.tensor_tensor(b, src, sin, ALU.mult))
                    nc.vector.tensor_tensor(dst[:, :, 0, :], ah[:, :, 0, :], bh[:, :, 1, :], ALU.subtract)
                    last = nc.vector.tensor_tensor(dst[:, :, 1, :], ah[:, :, 1, :], bh[:, :, 0, :], ALU.add)
                    if t == 0:
                        own(last)
                last.then_inc(acc_free, 1)
                dve.wait_ge(acc_free, n + 1)

            for n in range(1, 12):
                lo(2 * n)
                lo(2 * n + 1)
                if 0 <= n - 2 < 4:
                    rope(n - 2)
            lo(B_OUT)
            for h in range(HEADS):
                dve.wait_ge(qkT_done, 2 * h + 2)
                nc.vector.tensor_copy(kT[:, 2 * h:2 * h + 2, :],
                                      bank[QKT[2 * h + 1]][:, :].rearrange("p (c n) -> p c n", c=2)).then_inc(kTc, 1)
            dve.wait_ge(L["decay"], 16)

            def decayed(h):
                dve.wait_ge(s_ps, h + 1)
                if h >= 2:
                    dve.wait_ge(o_ps, 2 * (h - 2) + 2)
                nc.vector.tensor_tensor(S[:, h % 2, :], bank[6 + h % 2][:, 0:384], decay[:, h, :], ALU.mult).then_inc(s_sb, 1)

            def head(h):
                for t in range(TILES):
                    m = 2 * h + t
                    ob = bank[OB[h] + t][:, :]
                    dve.wait_ge(o_ps, m + 1)
                    own(nc.vector.bn_stats(stat[:, m, :], ob))
                    own(nc.vector.bn_aggr(mv[:, m, :], stat[:, m, :]))
                    if t == TILES - 1:
                        nc.vector.tensor_scalar(gr[:, 0, 2 * h:2 * h + 2], mv[:, 2 * h:2 * h + 2, 1], EPS, None,
                                                ALU.add).then_inc(gr_var, 1)
                for t in range(TILES):
                    m = 2 * h + t
                    nc.vector.scalar_tensor_tensor(o[:, h, t, :], bank[OB[h] + t][:, :], mv[:, m, 0:1], sg[:, h, t, :],
                                                   ALU.subtract, ALU.mult).then_inc(o_free, 1)

            def oTl_evac(h):
                for t in range(TILES):
                    dve.wait_ge(oTh_done, 2 * h + t + 1)
                    nc.vector.tensor_tensor(oTl[:, 4 * h:4 * h + 4, t * P:(t + 1) * P],
                                            bank[6 + t][:, :].rearrange("p (c n) -> p c n", c=4),
                                            oTh[:, 4 * h:4 * h + 4, t * P:(t + 1) * P].bitcast(f32),
                                            ALU.subtract).then_inc(oTl_done, 1)

            decayed(0)
            decayed(1)
            head(0)
            decayed(2)
            head(1)
            decayed(3)
            lo(B_OUT + 1)
            oTl_evac(0)
            head(2)
            lo(B_OUT + 2)
            lo(B_OUT + 3)
            oTl_evac(1)
            lo(B_OUT + 4)
            head(3)
            lo(B_OUT + 5)
            oTl_evac(2)
            lo(B_OUT + 6)
            lo(B_OUT + 7)
            oTl_evac(3)

            def residual(n, used, banks=DOWN):
                for t in range(TILES):
                    if t == 0:
                        dve.wait_ge(half_down, n)
                    else:
                        dve.wait_ge(pe_done, used)
                    for h in range(2):
                        cols = slice(h * BANK, (h + 1) * BANK)
                        last = nc.vector.tensor_tensor(res[:, t, cols], banks[t][h][:, :], res[:, t, cols], ALU.add)
                    last.then_inc(res_done, 1)

            lo(B_FFN)
            residual(1, B_FFN, DOWN_R)
            norm(1)
            xl_evac(1)
            lo(B_FFN + 1)

            def hidden(s, used, tiles):
                dve.wait_ge(pe_done, used)
                dve.wait_ge(silu_done, s + 1)
                for t in range(tiles):
                    last = nc.vector.tensor_tensor(hid[:, t, :], bank[2 + t][:, :], sgate[:, t, :], ALU.mult)
                last.then_inc(hid_done, 1)

            def hTl_evac(s, tiles):
                dve.wait_ge(hTh_done, s)
                for t in range(tiles):
                    last = nc.vector.tensor_tensor(hTl[:, :, t * P:(t + 1) * P],
                                                   bank[2 + t][:, :].rearrange("p (c n) -> p c n", c=4),
                                                   hTh[:, :, t * P:(t + 1) * P].bitcast(f32), ALU.subtract)
                last.then_inc(hTl_done, 1)

            def step(base, s, tiles, six=0, then=None, ahead=False):
                if not ahead:
                    lo(base, six)
                    lo(base + 1, six)
                hTl_evac(s, tiles)
                for b in range(2, 6):
                    lo(base + b, six)
                if then is not None:
                    then()
                hidden(s, base + 4 + 6 * six, tiles)

            def vl(c):
                dve.wait_ge(vh_done, c + 1)
                nc.vector.tensor_tensor(xl[:, c, :], y[:, c, :], xh[:, c, :].bitcast(f32), ALU.subtract).then_inc(vl_done, 1)

            for b in range(2, 6):
                lo(B_FFN + b)
                if b == 4:
                    hidden(0, B_FFN + 4, TILES)
            hTl_evac(1, TILES)
            for b in range(6, 10):
                lo(B_FFN + b)
            hidden(1, B_FFN + 8, TILES)
            with dve.Fori(0, STEPS - 2) as i:
                step(B_FFN + 10, i + 2, TILES, i)
            lo(B_PW1 - 2)
            lo(B_PW1 - 1)
            hTl_evac(STEPS, TILES)
            lo(B_PW1)
            residual(2, B_PW1)
            norm(2)
            xl_evac(2)
            for b in range(1, 5):
                lo(B_PW1 + b)
            dve.wait_ge(L["bias1"], 16)

            def glu(half):
                cols, gcols = slice(half * BANK, (half + 1) * BANK), slice(D + half * BANK, D + (half + 1) * BANK)
                dve.wait_ge(pe_done, B_PW1 + 4 * half + 4)
                for t in range(TILES):
                    nc.vector.tensor_tensor(ug[:, t, cols], bank[4 * half + 2 + t][:, :], bias1[:, gcols],
                                            ALU.add).then_inc(a_gate, 1)
                for t in range(TILES):
                    last = nc.vector.tensor_tensor(ua[:, t, cols], bank[4 * half + t][:, :], bias1[:, cols], ALU.add)
                own(last)
                for t in range(TILES):
                    dve.wait_ge(sig_done, 2 * half + t + 1)
                    nc.vector.tensor_tensor(ua[:, t, cols], ua[:, t, cols], ug[:, t, cols], ALU.mult).then_inc(u_done, 1)

            glu(0)
            for b in range(5, 8):
                lo(B_PW1 + b)
            dve.wait_ge(small_sb, 2)
            dve.wait_ge(pad_set, 1)
            dve.wait_ge(uT_sb, 2)
            done = {c: 0 for c in range(5)}
            count = [0]

            def tap(c, k):
                if k:
                    dve.wait_ge(tap_seq, done[c])
                w = wdwT[:, k * DC + c:k * DC + c + 1]
                if k == 0:
                    ins = nc.vector.tensor_scalar(y[:, c, :], uT[:, c, 0:SEQ], w, smallT[:, c:c + 1], ALU.mult, ALU.add)
                else:
                    ins = nc.vector.scalar_tensor_tensor(y[:, c, :], uT[:, c, k:k + SEQ], w, y[:, c, :], ALU.mult, ALU.add)
                ins.then_inc(tap_seq, 1)
                count[0] += 1
                done[c] = count[0]

            for k in range(EARLY_TAPS):
                for c in range(4):
                    tap(c, k)
            glu(1)
            for b in range(3):
                lo(B_PW2 + b)
            dve.wait_ge(uT_sb, 4)
            for k in range(EARLY_TAPS, TAPS):
                for c in range(4):
                    tap(c, k)
                if k - EARLY_TAPS < SPLIT_TAP:
                    tap(4, k - EARLY_TAPS)
            dve.wait_ge(tap_seq, count[0])
            dve.wait_ge(tap_done, TAPS - SPLIT_TAP)
            nc.vector.tensor_tensor(y[:, 4, :], bank[4][:, 0:SEQ], y[:, 4, :], ALU.add).then_inc(y_done, 1)
            dve.wait_ge(mu_ps, 1)
            own(nc.vector.tensor_scalar(stats2[:, 0, :], bank[0][:, 0:SEQ], 1.0 / D, None, ALU.mult))
            for c in range(DC):
                nc.vector.tensor_tensor(y[:, c, :], y[:, c, :], stats2[:, 0, :], ALU.subtract).then_inc(yc_done, 1)
            dve.wait_ge(var_ps, 1)
            nc.vector.tensor_scalar(stats2[:, 1, :], bank[1][:, 0:SEQ], 1.0 / D, EPS, ALU.mult, ALU.add).then_inc(var_sb, 1)
            dve.wait_ge(std_done, 1)
            own(nc.vector.reciprocal(stats2[:, 0, :], stats2[:, 2, :]))
            own(nc.vector.tensor_tensor(stats2[:, 2, :], stats2[:, 0, :], stats2[:, 0, :], ALU.mult))
            own(nc.vector.scalar_tensor_tensor(stats2[:, 2, :], stats2[:, 2, :], -0.5, stats2[:, 1, :], ALU.mult, ALU.mult))
            own(nc.vector.scalar_tensor_tensor(stats2[:, 3, :], stats2[:, 2, :], 1.5, stats2[:, 0, :], ALU.add, ALU.mult))
            for c in range(DC):
                nc.vector.tensor_tensor(y[:, c, :], y[:, c, :], stats2[:, 3, :], ALU.mult).then_inc(yn_done, 1)
                if c >= 2:
                    vl(c - 2)
            for c in range(DC - 2, DC):
                vl(c)
            lo(B_PW2 + 3)
            dve.wait_ge(L["bias2"], 16)
            for t in range(TILES):
                last = nc.vector.tensor_tensor(res[:, t, :], res[:, t, :], bias2[:, :], ALU.add)
            own(last)
            lo(B_MOE)
            residual(3, B_MOE)
            norm(3)
            for t in range(TILES):
                dve.wait_ge(zT_done, 12 + 2 * t + 2)
                nc.vector.tensor_copy(hT32[:, 4:8, t * P:(t + 1) * P],
                                      bank[2 * t + 1][:, :].rearrange("p (c n) -> p c n", c=4)).then_inc(hT32b_done, 1)
            lo(B_MOE + 1)
            for t in range(TILES):
                dve.wait_ge(zh_done, t + 1)
                nc.vector.tensor_tensor(zl[:, t, :], z[:, t, :], zh[:, t, :].bitcast(f32), ALU.subtract).then_inc(zl_done, 1)

            dve.wait_ge(L["route"], 16)
            dve.wait_ge(lg_ps, 1)
            own(nc.vector.tensor_copy(lg[:, :, :], bank[4][:, 0:TILES * NE].rearrange("p (t e) -> p t e", t=TILES)))
            before = route[:, :].rearrange("p (a b) -> p a b", a=NE)
            for t in range(TILES):
                le = lg[:, t, :].unsqueeze(2).to_broadcast([P, NE, NE])
                lf = lg[:, t, :].unsqueeze(1).to_broadcast([P, NE, NE])
                nc.vector.tensor_tensor(w64[:, 0, t, :].rearrange("p (a b) -> p a b", a=NE), lf, le, ALU.is_gt)
                last = nc.vector.tensor_tensor(w64[:, 1, t, :].rearrange("p (a b) -> p a b", a=NE), lf, le, ALU.is_equal)
            own(last)
            own(nc.vector.tensor_tensor(w64[:, 1, :, :], w64[:, 1, :, :],
                                        route[:, :].unsqueeze(1).to_broadcast([P, TILES, 64]), ALU.mult))
            own(nc.vector.tensor_tensor(w64[:, 0, :, :], w64[:, 0, :, :], w64[:, 1, :, :], ALU.add))
            own(nc.vector.reduce_sum(rk[:, 1, :, :], w64[:, 0, :, :].rearrange("p t (a b) -> p t a b", a=NE), AX.X))
            own(nc.vector.tensor_scalar(rk[:, 2, :, :], rk[:, 1, :, :], 1.5, None, ALU.is_lt))
            nc.vector.tensor_copy(rk[:, 4, :, :], rk[:, 2, :, :]).then_inc(sel_done, 1)
            for t in range(TILES):
                own(nc.vector.max(srt[:, t, :], lg[:, t, :]))
                last = nc.vector.tensor_scalar(rk[:, 7, t, :], lg[:, t, :], srt[:, t, 0:1], None, ALU.subtract)
            last.then_inc(lg_max, 1)
            dve.wait_ge(rank_ps, 1)
            pref = bank[5][:, 0:TILES * NE].rearrange("p (t e) -> p t e", t=TILES)
            own(nc.vector.scalar_tensor_tensor(rk[:, 5, :, :], pref, 1.0, rk[:, 2, :, :], ALU.add, ALU.mult))
            nc.vector.tensor_scalar(tot[:, 1, :], bank[5][:, 2 * NE:3 * NE], P + 0.5, None, ALU.is_gt)
            for s in range(2):
                last = nc.vector.tensor_scalar(slot[:, s, :, :], rk[:, 5, :, :], -1.0 - s * P, None, ALU.add)
            own(last)
            nc.vector.tensor_copy(twoi[:, :], tot[:, 1, :]).then_inc(two_done, 1)

            def build_onehot(e):
                for s in range(2):
                    for t in range(TILES):
                        last = nc.vector.tensor_scalar(onehot[:, t, s * P:(s + 1) * P], iota, slot[:, s, t, bass.ds(e, 1)], None,
                                                       ALU.is_equal)
                last.then_inc(onehot_done, 1)

            def xel_evac(e, half, tiles=2):
                dve.wait_ge(xeh_done, 2 * e + half + 1)
                for q in range(2):
                    chunks = slice(4 * half + 2 * q, 4 * half + 2 * q + 2)
                    last = nc.vector.tensor_tensor(xl[:, chunks, :],
                                                   gather_banks(half, tiles)[q][:, :].rearrange("p (c n) -> p c n", c=2),
                                                   xh[:, chunks, :].bitcast(f32), ALU.subtract)
                last.then_inc(xel_done, 1)

            build_onehot(0)
            dve.wait_ge(ex_done, 1)
            own(nc.vector.tensor_tensor(rk[:, 3, :, :], rk[:, 0, :, :], rk[:, 2, :, :], ALU.mult))
            own(nc.vector.reduce_sum(tot[:, 0, 0:TILES], rk[:, 3, :, :], AX.X))
            xel_evac(0, 0)
            own(nc.vector.reciprocal(tot[:, 0, 2:2 + TILES], tot[:, 0, 0:TILES]))
            for t in range(TILES):
                last = nc.vector.tensor_scalar(comb[:, t, :], rk[:, 3, t, :], tot[:, 0, 2 + t:3 + t], None, ALU.mult)
            own(last)
            lo(B_MOE + 2)
            xel_evac(0, 1)
            lo(B_MOE + 3)
            dve.wait_ge(two_done, 1)
            both(dve, needs_two(dve, 0), lambda tiles: hidden(STEPS, B_MOE + 4, tiles))

            def y_lo(e, two):
                def piece(tiles):
                    dve.wait_ge(yh_done, e + 1)
                    for s in range(tiles):
                        for n in range(2):
                            cols = slice(n * BANK, (n + 1) * BANK)
                            last = nc.vector.tensor_tensor(yl[:, s, cols], DOWN[s][n][:, :], yh[:, s, cols].bitcast(f32),
                                                           ALU.subtract)
                    last.then_inc(yl_done, 1)

                both(dve, two, piece)

            def accumulate(e):
                dve.wait_ge(scat_ps, e + 1)
                for t in range(TILES):
                    for n in range(2):
                        cols = slice(n * BANK, (n + 1) * BANK)
                        last = nc.vector.scalar_tensor_tensor(res[:, t, cols], SCAT[2 * t + n][:, :],
                                                              comb[:, t, bass.ds(e, 1)], res[:, t, cols],
                                                              ALU.mult, ALU.add)
                    last.then_inc(res_done, 1)

            def next_onehot(e):
                dve.wait_ge(ohT_ps, e + 1)
                build_onehot(e + 1)

            def expert_steps(e, two, last=False):
                s0, six0 = STEPS * e + (STEPS + 1), STEPS * e

                def piece(tiles):
                    step(B_MOE + 4, s0, tiles, six0, None if last else lambda: next_onehot(e), ahead=True)
                    with dve.Fori(0, STEPS - 3) as i:
                        step(B_MOE + 10, s0 + 1 + i, tiles, six0 + i)
                    step(B_MOE + 34, s0 + 5, tiles, six0, None if last else lambda: xel_evac(e + 1, 0))

                both(dve, two, piece)

            lo(B_MOE + 4)
            lo(B_MOE + 5)
            with dve.Fori(0, NE - 1) as e:
                two, two_next = needs_two(dve, e), needs_two(dve, e + 1)
                expert_steps(e, two)
                s, six = STEPS * e + 2 * STEPS, STEPS * e + (STEPS - 1)
                lo(B_MOE + 4, six)
                both(dve, two, lambda tiles: xel_evac(e + 1, 1, tiles))
                lo(B_MOE + 5, six)
                both(dve, two, lambda tiles: hTl_evac(s, tiles))
                for b in range(6, 10):
                    lo(B_MOE + b, six)
                y_lo(e, two)
                both(dve, two_next, lambda tiles: hidden(s, B_MOE + 10 + 6 * six, tiles))
                lo(B_MOE + 10, six)
                lo(B_MOE + 11, six)
                accumulate(e)
            two = needs_two(dve, NE - 1)
            expert_steps(NE - 1, two, last=True)
            six = STEPS * NE - 1
            lo(B_MOE + 4, six)
            lo(B_MOE + 5, six)
            both(dve, two, lambda tiles: hTl_evac(STEPS * NE + STEPS, tiles))
            y_lo(NE - 1, two)
            accumulate(NE - 1)
            norm(4)

        @block.tensor
        def _(pe):
            def product(dst, ah, al, bh, bl, start, stop):
                nc.tensor.matmul(dst, ah, bh, start=start, stop=False)
                nc.tensor.matmul(dst, ah, bl, start=False, stop=False)
                return nc.tensor.matmul(dst, al, bh, start=False, stop=stop)

            def columns(base, acc, half, ready=None, tiles=TILES, six=0):
                pe.wait_ge(lo_done, base + 1 + 6 * six)
                slot_ = base % SPLIT
                for t in range(tiles):
                    if ready is not None:
                        pe.wait_ge(xl_done, ready + 2 * t + 2)
                    for c in range(4):
                        kc = 4 * half + c
                        tok = slice(t * P, (t + 1) * P)
                        last = product(acc[t][:, :], xh[:, kc, tok], xl[:, kc, tok],
                                       whi[slot_][:, c * BANK:(c + 1) * BANK], wlo[slot_][:, c * BANK:(c + 1) * BANK],
                                       kc == 0, kc == DC - 1)
                last.then_inc(pe_done, 1)

            def rows(base, ah, al, first_chunk, start, stop, tiles=TILES, six=0, banks=DOWN, halves=True):
                pe.wait_ge(lo_done, base + 1 + 6 * six)
                slot_ = base % SPLIT
                for t in range(tiles):
                    for c in range(2):
                        kc = first_chunk + c
                        tok = slice(t * P, (t + 1) * P)
                        for n in range(2):
                            col = c * D + n * BANK
                            last = product(banks[t][n][:, :], ah[:, kc, tok], al[:, kc, tok],
                                           whi[slot_][:, col:col + BANK], wlo[slot_][:, col:col + BANK],
                                           start and c == 0, stop and c == 1)
                    if stop and t == 0 and halves:
                        last.then_inc(half_down, 1)
                last.then_inc(pe_done, 1)

            def turn(k):
                for t in range(TILES):
                    pe.wait_ge(z_done, 2 * k + t + 1)
                    for c in range(DC):
                        last = nc.tensor.transpose(bank[2 * t + c // 4][:, c % 4 * P:(c % 4 + 1) * P],
                                                   z[:, t, c * P:(c + 1) * P], ident)
                        if c % 4 == 3:
                            last.then_inc(zT_done, 1)

            pe.wait_ge(L["mats"], 16)
            pe.wait_ge(L["wdw"], 16)
            pe.wait_ge(L["small"], 48)
            for a in range(2):
                nc.tensor.transpose(bank[4][:, a * 124:(a + 1) * 124], wdw[:, a, :], ident[0:124, 0:124])
            nc.tensor.transpose(bank[4][:, 256:280], small[:, :], ident[0:24, 0:24]).then_inc(small_ps, 1)
            turn(0)
            for n in range(3):
                if n == 2:
                    pe.wait_ge(small_sb, 2)
                for half in range(2):
                    columns(2 * n + half, bank[2 * n:2 * n + 2], half, 0 if n == 0 else None)
            with pe.Fori(0, 3) as i:
                for n in range(3):
                    pe.wait_ge(acc_free, 3 * i + n + 1)
                    for half in range(2):
                        columns(6 + 2 * n + half, bank[2 * n:2 * n + 2], half, six=i)
            for m in range(8):
                h = m // 2
                pe.wait_ge(acc_free, (4, 4, 10, 10, 11, 11, 12, 12)[m])
                for cc in range(2):
                    c = 2 * h + cc
                    for t in range(TILES):
                        last = nc.tensor.transpose(bank[QKT[m]][:, cc * SEQ + t * P:cc * SEQ + (t + 1) * P],
                                                   qk[:, m % 2, t, c * P:(c + 1) * P], ident)
                last.then_inc(qkT_done, 1)

            def scores(h):
                pe.wait_ge(qTc, h + 1)
                pe.wait_ge(kTc, h + 1)
                if h >= 2:
                    pe.wait_ge(s_sb, h - 1)
                dst = bank[6 + h % 2]
                for dc in range(2):
                    nc.tensor.matmul(dst[:, 0:SEQ], kT[:, 2 * h + dc, 0:P], qT[:, 2 * h + dc, :],
                                     start=dc == 0, stop=dc == 1)
                for dc in range(2):
                    last = nc.tensor.matmul(dst[:, SEQ:384], kT[:, 2 * h + dc, P:SEQ], qT[:, 2 * h + dc, P:SEQ],
                                            start=dc == 0, stop=dc == 1)
                last.then_inc(s_ps, 1)

            def values(h):
                pe.wait_ge(s_sb, h + 1)
                if h == 0:
                    pe.wait_ge(qTc, 2)
                    pe.wait_ge(kTc, 2)
                elif h == 1:
                    pe.wait_ge(qTc, 3)
                    pe.wait_ge(kTc, 3)
                elif h == 2:
                    pe.wait_ge(o_free, 2)
                else:
                    pe.wait_ge(o_free, 6)
                dst = bank[OB[h]]
                nc.tensor.matmul(dst[:, :], S[:, h % 2, 0:P], v[:, h, 0, :], start=True, stop=True).then_inc(o_ps, 1)
                dst = bank[OB[h] + 1]
                nc.tensor.matmul(dst[:, :], S[:, h % 2, P:SEQ], v[:, h, 0, :], start=True, stop=False)
                nc.tensor.matmul(dst[:, :], S[:, h % 2, SEQ:384], v[:, h, 1, :], start=False, stop=True).then_inc(o_ps, 1)

            def o_turn(h):
                pe.wait_ge(s_sb, 4)
                if h:
                    pe.wait_ge(oTl_done, 2 * h)
                for t in range(TILES):
                    pe.wait_ge(gated, 2 * h + t + 1)
                    for c in range(4):
                        last = nc.tensor.transpose(bank[6 + t][:, c * P:(c + 1) * P], o[:, h, t, c * P:(c + 1) * P], ident)
                    last.then_inc(oT_ps, 1)

            def project(r):
                pe.wait_ge(oTl_done, 2 * (r // 2) + 2)
                if r == 0:
                    pe.wait_ge(o_free, 4)
                    pe.wait_ge(kTc, 4)
                    pe.wait_ge(qTc, 4)
                rows(B_OUT + r, oTh, oTl, 2 * r, r == 0, r == 7, banks=DOWN_R)

            scores(0)
            scores(1)
            values(0)
            scores(2)
            values(1)
            scores(3)
            o_turn(0)
            values(2)
            project(0)
            o_turn(1)
            project(1)
            values(3)
            project(2)
            o_turn(2)
            project(3)
            project(4)
            o_turn(3)
            for r in range(5, 8):
                project(r)

            def hT_turn(s, tiles, shared=None):
                pe.wait_ge(hid_done, s + 1)
                for t in range(tiles):
                    for c in range(4):
                        if shared is not None and t == tiles - 1 and c == 3:
                            pe.wait_ge(xel_done, shared)
                        last = nc.tensor.transpose(bank[2 + t][:, c * P:(c + 1) * P], hid[:, t, c * P:(c + 1) * P], ident)
                last.then_inc(hT_ps, 1)

            def step(base, s, tiles, first=False, six=0, between=None, then=None, shared=None):
                pe.wait_ge(silu_done, s)
                columns(base, bank[0:2], 0, tiles=tiles, six=six)
                columns(base + 1, bank[0:2], 1, tiles=tiles, six=six)
                pe.wait_ge(hTl_done, s)
                columns(base + 2, bank[2:4], 0, tiles=tiles, six=six)
                columns(base + 3, bank[2:4], 1, tiles=tiles, six=six)
                if between is not None:
                    pe.wait_ge(silu_done, s + 1)
                    between()
                rows(base + 4, hTh, hTl, 0, first, False, tiles, six)
                rows(base + 5, hTh, hTl, 2, False, False, tiles, six)
                if then is not None:
                    then()
                hT_turn(s, tiles, shared)

            turn(1)
            pe.wait_ge(xl_done, 6)
            for half in range(2):
                columns(B_FFN + half, bank[0:2], half, 4)
            for half in range(2):
                columns(B_FFN + 2 + half, bank[2:4], half)
            hT_turn(0, TILES)
            pe.wait_ge(res_done, 2)
            step(B_FFN + 4, 1, TILES, True)
            with pe.Fori(0, STEPS - 2) as i:
                step(B_FFN + 10, i + 2, TILES, six=i)
            pe.wait_ge(hTl_done, STEPS)
            rows(B_PW1 - 2, hTh, hTl, 0, False, False)
            rows(B_PW1 - 1, hTh, hTl, 2, False, True)

            turn(2)
            pe.wait_ge(xl_done, 10)

            def u_turn(half):
                for t in range(TILES):
                    pe.wait_ge(u_done, 2 * half + t + 1)
                    for c in range(4):
                        col = half * BANK + c * P
                        last = nc.tensor.transpose(bank[4 * half + t][:, c * P:(c + 1) * P], ua[:, t, col:col + P], ident)
                    last.then_inc(uT_ps, 1)

            for b in range(8):
                n = b // 2
                columns(B_PW1 + b, bank[2 * n:2 * n + 2], b % 2, 8 if n == 0 else None)
                if b == 4:
                    u_turn(0)
            u_turn(1)
            pe.wait_ge(uT_sb, 4)
            pe.wait_ge(pad_set, 1)
            for m, (c, k) in enumerate(PE_TAPS):
                pe.wait_ge(diag_done, m + 1)
                last = nc.tensor.matmul(bank[c][:, 0:SEQ], diag[:, m % 8, :], uT[:, c, k:k + SEQ],
                                        start=k == (SPLIT_TAP if c == 4 else 0), stop=k == TAPS - 1)
                last.then_inc(tap_done, 1)
            for n, c in enumerate((5, 6, 0, 1, 2, 3, 4, 7)):
                if c >= 5:
                    pe.wait_ge(y_pe, c - 4)
                else:
                    pe.wait_ge(y_done, 1)
                last = nc.tensor.matmul(bank[0][:, 0:SEQ], ones, y[:, c, :], start=n == 0, stop=n == DC - 1)
            last.then_inc(mu_ps, 1)
            for c in range(DC):
                pe.wait_ge(sq_done, c + 1)
                last = nc.tensor.matmul(bank[1][:, 0:SEQ], ones, sq[:, c, :], start=c == 0, stop=c == DC - 1)
            last.then_inc(var_ps, 1)
            for r in range(4):
                pe.wait_ge(vl_done, 2 * r + 2)
                rows(B_PW2 + r, xh, xl, 2 * r, r == 0, r == 3)

            turn(3)
            pe.wait_ge(res_done, 6)
            pe.wait_ge(L["wr"], 16)
            for t in range(TILES):
                pe.wait_ge(hT32_done, t + 1)
                pe.wait_ge(hT32b_done, t + 1)
                for c in range(DC):
                    last = nc.tensor.matmul(bank[4][:, t * NE:(t + 1) * NE], hT32[:, c, t * P:(t + 1) * P], wr[:, c, :],
                                            start=c == 0, stop=c == DC - 1)
            last.then_inc(lg_ps, 1)
            pe.wait_ge(sel_done, 1)
            nc.tensor.matmul(bank[5][:, 0:NE], earlier, rk[:, 4, 0, :], start=True, stop=True)
            nc.tensor.matmul(bank[5][:, NE:2 * NE], earlier, rk[:, 4, 1, :], start=True, stop=False)
            nc.tensor.matmul(bank[5][:, NE:2 * NE], ones, rk[:, 4, 0, :], start=False, stop=True)
            nc.tensor.matmul(bank[5][:, 2 * NE:3 * NE], ones, rk[:, 4, 0, :], start=True, stop=False)
            nc.tensor.matmul(bank[5][:, 2 * NE:3 * NE], ones, rk[:, 4, 1, :], start=False, stop=True).then_inc(rank_ps, 1)

            def gather(e, half, tiles=2):
                pe.wait_ge(onehot_done, e + 1)
                if half and tiles == 2:
                    pe.wait_ge(xel_done, 2 * e + 1)
                for c in range(4):
                    dst = gather_banks(half, tiles)[c // 2][:, c % 2 * SEQ:(c % 2 + 1) * SEQ]
                    col = half * BANK + c * P
                    for t in range(TILES):
                        nc.tensor.matmul(dst, zh[:, t, col:col + P], onehot[:, t, :], start=t == 0, stop=False)
                        last = nc.tensor.matmul(dst, zl[:, t, col:col + P], onehot[:, t, :], start=False,
                                                stop=t == TILES - 1)
                last.then_inc(gather_ps, 1)

            def onehot_turn(e):
                for s in range(2):
                    for t in range(TILES):
                        last = nc.tensor.matmul(bank[0][:, s * SEQ + t * P:s * SEQ + (t + 1) * P],
                                                onehot[:, t, s * P:(s + 1) * P],
                                                identr[:, :], start=True, stop=True)
                last.then_inc(ohT_ps, 1)
                pe.wait_ge(res_done, 2 * e + 6)

            def scatter(e, two):
                def piece(tiles):
                    pe.wait_ge(yl_done, e + 1)
                    for t in range(TILES):
                        for n in range(2):
                            dst, cols = SCAT[2 * t + n][:, :], slice(n * BANK, (n + 1) * BANK)
                            for s in range(tiles):
                                where = onehotT[:, s, t * P:(t + 1) * P]
                                nc.tensor.matmul(dst, where, yh[:, s, cols], start=s == 0, stop=False)
                                last = nc.tensor.matmul(dst, where, yl[:, s, cols], start=False, stop=s == tiles - 1)
                    last.then_inc(scat_ps, 1)

                both(pe, two, piece)

            def gates(base, two, e, s, six=0):
                def piece(half, tiles):
                    pe.wait_ge(silu_done, s)
                    pe.wait_ge(xel_done, 2 * e + half + 1)
                    columns(base + half, bank[0:2], half, tiles=tiles, six=six)

                both(pe, two, lambda tiles: piece(0, tiles))
                both(pe, two, lambda tiles: piece(1, tiles))

            def ups(base, two, six=0):
                for half in range(2):
                    both(pe, two, lambda tiles: columns(base + half, bank[2:4], half, tiles=tiles, six=six))

            def expert_steps(e, two, last=False):
                s0, six0 = STEPS * e + (STEPS + 1), STEPS * e

                def piece(tiles):
                    step(B_MOE + 4, s0, tiles, True, six0, between=lambda: onehot_turn(e),
                         then=lambda: pe.wait_ge(ohT_done, e + 1))
                    with pe.Fori(0, STEPS - 3) as i:
                        step(B_MOE + 10, s0 + 1 + i, tiles, six=six0 + i)
                    if last:
                        step(B_MOE + 34, s0 + 5, tiles, six=six0)
                    elif tiles == 1:
                        step(B_MOE + 34, s0 + 5, 1, six=six0, between=lambda: (gather(e + 1, 0), gather(e + 1, 1, 1)))
                    else:
                        step(B_MOE + 34, s0 + 5, 2, six=six0, between=lambda: gather(e + 1, 0),
                             then=lambda: gather(e + 1, 1), shared=2 * e + 4)

                both(pe, two, piece)

            def last_rows(base, two, s, six):
                def piece(r, tiles):
                    pe.wait_ge(hTl_done, s)
                    rows(base + r, hTh, hTl, 2 * r, False, r == 1, tiles, six, halves=False)

                both(pe, two, lambda tiles: piece(0, tiles))
                both(pe, two, lambda tiles: piece(1, tiles))

            pe.wait_ge(zh_done, 3)
            pe.wait_ge(zl_done, 2)
            gather(0, 0)
            gather(0, 1)
            pe.wait_ge(two_done, 1)
            pe.wait_ge(xel_done, 2)
            two = needs_two(pe, 0)
            gates(B_MOE, two, 0, STEPS)
            ups(B_MOE + 2, two)
            both(pe, two, lambda tiles: hT_turn(STEPS, tiles))

            with pe.Fori(0, NE - 1) as e:
                two, two_next = needs_two(pe, e), needs_two(pe, e + 1)
                expert_steps(e, two)
                s, six = STEPS * e + 2 * STEPS, STEPS * e + (STEPS - 1)
                gates(B_MOE + 4, two_next, e + 1, s, six)
                last_rows(B_MOE + 6, two, s, six)
                ups(B_MOE + 8, two_next, six)
                scatter(e, two)
                both(pe, two_next, lambda tiles: hT_turn(s, tiles))
            two = needs_two(pe, NE - 1)
            expert_steps(NE - 1, two, last=True)
            last_rows(B_MOE + 4, two, STEPS * NE + STEPS, STEPS * NE - 1)
            scatter(NE - 1, two)


def constants():
    f = np.float32
    i = np.arange(P)
    mats = np.zeros((P, 4, P), f)
    mats[:, 0] = np.eye(P)
    mats[:, 1] = i[:, None] < i[None, :]
    mats[:, 2] = 1
    mats[:, 3] = i[None, :]
    half = DQK // 2
    freq = (f(10000.0) ** (-np.arange(half, dtype=f) / f(half))).astype(f)
    lg = np.log1p(-(2.0 ** (-5.0 - np.arange(HEADS, dtype=np.float64))))
    rel = i[None, :] - i[:, None]
    decay = np.zeros((P, HEADS, 3, P), np.float64)
    for h in range(HEADS):
        same = np.where(rel >= 0, np.exp(np.maximum(rel, 0) * lg[h]), 0.0)
        cross = np.exp((i[None, :] + 1 + P - 1 - i[:, None]) * lg[h])
        decay[:, h] = np.stack([same, cross, same], 1) * DQK ** -0.5
    e = np.arange(NE)
    route = (e[None, :] < e[:, None]).reshape(-1).astype(f)
    return {"c_mats": mats, "c_freq": freq, "c_decay": decay.reshape(P, HEADS, 384).astype(f), "c_route": route}


INPUTS = ["x", "positions", "norm_mix_g", "norm_ffn_g", "final_norm_g", "ret_w_in", "ret_w_out", "conv_w_pw1",
          "conv_b_pw1", "conv_w_dw", "conv_b_dw", "conv_ln_g", "conv_ln_b", "conv_w_pw2", "conv_b_pw2", "ffn_w_gu",
          "ffn_w_down", "moe_w_router", "moe_w_gu", "moe_w_down"]


def kernel(**inputs):
    import concourse.bacc as bacc
    from concourse.bass_utils import run_bass_kernel_spmd

    nc = bacc.Bacc("TRN2", target_bir_lowering=False, num_devices=1)
    arrays, args = {}, []
    for name, a in [(n, inputs[n]) for n in INPUTS] + list(constants().items()):
        a = np.ascontiguousarray(a)
        arrays[f"in_{name}"] = a
        args.append(nc.dram_tensor(f"in_{name}", a.shape, mybir.dt.from_np(a.dtype), kind="ExternalInput").ap())
    args.append(nc.dram_tensor("out_h", (1, SEQ, D), mybir.dt.float32, kind="ExternalOutput").ap())
    trunk(nc, *args)
    r = run_bass_kernel_spmd(nc, [arrays], core_ids=[0])
    return r.results[0]["out_h"]
```

```python
import numpy as np
import concourse.bass as bass
from concourse import mybir
from contextlib import ExitStack

SEQ, D, P = 256, 1024, 128
TILES = SEQ // P
HEADS, DQK, DV = 4, 256, 512
FF, NE = 3584, 8
TAPS = 31
EPS = 1e-6
BANK = 512
DC = D // P
RAW, SPLIT = 6, 3
BLK = 2048
STEPS = FF // BANK
STEP_BLOCKS = 6
B_OUT = 2 * (6 * D // BANK)
B_FFN = B_OUT + 2 * D // 256
B_PW1 = B_FFN + STEPS * STEP_BLOCKS
B_PW2 = B_PW1 + 8
B_MOE = B_PW2 + 4
PAD = TAPS - 1
ONE, TWO, PACKED = 1, 2, 3
HALF = P // 2
EARLY_TAPS = 7
VECTOR_TAPS = {0: TAPS, 1: TAPS, 2: TAPS, 3: 22, 4: 21}


def trunk(nc, x, positions, norm_mix_g, norm_ffn_g, final_norm_g, ret_w_in, ret_w_out, conv_w_pw1,
          conv_b_pw1, conv_w_dw, conv_b_dw, conv_ln_g, conv_ln_b, conv_w_pw2, conv_b_pw2, ffn_w_gu,
          ffn_w_down, moe_w_router, moe_w_gu, moe_w_down, c_mats, c_freq, c_decay, c_route, out):
    f32, f32r, i32 = mybir.dt.float32, mybir.dt.float32r, mybir.dt.int32
    ALU, ACT, AX = mybir.AluOpType, mybir.ActivationFunctionType, mybir.AxisListType

    ctx = ExitStack()
    with ctx:
        ctx.enter_context(nc.allow_non_contiguous_dma(reason="small vectors"))
        cursor = [(nc.sbuf_base + 63) // 64 * 64]

        def at(name, shape, dt, where=None):
            size = int(np.prod(shape[1:])) * 4
            off = cursor[0] if where is None else where
            if where is None:
                cursor[0] += (size + 63) // 64 * 64
            assert off + size <= nc.sbuf_usable_end, (name, off + size)
            return nc.alloc_sbuf_tensor_at(name, shape, dt, offset=off)

        raw = [at(f"raw{i}", [P, BLK], f32) for i in range(RAW)]
        whi = [at(f"whi{i}", [P, BLK], f32r) for i in range(SPLIT)]
        wlo = [at(f"wlo{i}", [P, BLK], f32r) for i in range(SPLIT)]
        res = at("res", [P, TILES, D], f32)
        z_at = cursor[0]
        z = at("z", [P, TILES, D], f32)
        xt_at = cursor[0]
        xh = at("xh", [P, DC, SEQ], f32r)
        xl = at("xl", [P, DC, SEQ], f32r)
        gains_at = cursor[0]
        gains = at("gains", [P, 2, D], f32)
        mats = at("mats", [P, 4, P], f32)
        ident, earlier, ones, iota = (mats[:, i, :] for i in range(4))
        small = at("small", [24, P], f32)
        smallT = at("smallT", [P, 24], f32)
        wdw = at("wdw", [124, 2, P], f32)
        wdwT = at("wdwT", [P, TAPS * DC], f32)
        ss = at("ss", [P, 2], f32)
        ms = at("ms", [P, 2], f32)
        rstd = at("rstd", [P, 2], f32)
        lnv = at("lnv", [P, 2, 2], f32)
        mhalf = at("mhalf", [P, 8], f32)
        stage_at = cursor[0]

        o_at = stage_at
        qk = at("qk", [P, 2, TILES, D], f32, o_at)
        o = at("o", [P, HEADS, TILES, DV], f32, o_at)
        qT = at("qT", [P, 2 * HEADS, SEQ], f32, xt_at)
        kT = at("kT", [P, 2 * HEADS, SEQ], f32, xt_at + 8192)
        oTl = at("oTl", [P, 16, SEQ], f32r, xt_at)
        v_at = o_at + 16384
        v = at("v", [P, HEADS, TILES, DV], f32, v_at)
        oTh = at("oTh", [P, 16, SEQ], f32r, v_at)
        sg = at("sg", [P, HEADS, TILES, DV], f32, v_at + 16384)
        r_at = v_at + 32768
        decay = at("decay", [P, HEADS, 384], f32, r_at)
        cs = at("cs", [P, 2, TILES, P], f32, r_at + 6144)
        ang = at("ang", [P, 3, TILES, P], f32, r_at + 8192)
        S = at("S", [P, 2, 384], f32, r_at + 8192)
        stat = at("stat", [P, 8, 6], f32, r_at + 11264)
        mv = at("mv", [P, 8, 2], f32, r_at + 11520)
        gr = at("gr", [P, 2, 8], f32, r_at + 11648)
        posi = at("posi", [P, TILES], i32, r_at + 11776)
        posf = at("posf", [P, TILES], f32, r_at + 11840)
        tmp = at("tmp", [P, 2, BANK], f32, r_at + 11904)
        freq = at("freq", [P, P], f32, r_at + 16000)

        hTh = at("hTh", [P, 4, SEQ], f32r, stage_at)
        hTl = at("hTl", [P, 4, SEQ], f32r, stage_at + 4096)
        sgate = at("sgate", [P, TILES, BANK], f32, stage_at + 8192)
        hid = at("hid", [P, TILES, BANK], f32, stage_at + 12288)
        conv_at = stage_at + 16384
        ua = at("ua", [P, TILES, D], f32, conv_at)
        ug = at("ug", [P, TILES, D], f32, conv_at + 8192)
        y = at("y", [P, DC, SEQ], f32, z_at)
        sq = at("sq", [P, DC, SEQ], f32, conv_at + 8192)
        uT = at("uT", [P, DC, PAD + SEQ], f32, conv_at + 16384)
        bias1 = at("bias1", [P, 2 * D], f32, conv_at + 16384 + 9152)
        bias2 = at("bias2", [P, D], f32, conv_at + 16384 + 9152 + 8192)
        mean = at("mean", [P, SEQ], f32, conv_at + 16384 + 9152 + 12288)
        diag = at("diag", [P, 8, P], f32, stage_at + 8192)
        zh = at("zh", [P, TILES, D], f32r, conv_at)
        zl = at("zl", [P, TILES, D], f32r, conv_at + 8192)
        hT32 = at("hT32", [P, DC, SEQ], f32, conv_at + 16384)
        m_at = conv_at + 24576
        yh = at("yh", [P, 2, D], f32r, m_at)
        yl = at("yl", [P, 2, D], f32r, m_at + 8192)
        onehot = at("onehot", [P, TILES, 2 * P], f32r, m_at + 16384)
        onehotT = at("onehotT", [P, 2, SEQ], f32r, m_at + 18432)
        identr = at("identr", [P, P], f32r, m_at + 20480)
        wr = at("wr", [P, DC, NE], f32, m_at + 20992)
        route = at("route", [P, NE * NE], f32, m_at + 21248)
        lg = at("lg", [P, TILES, NE], f32, m_at + 21504)
        srt = at("srt", [P, TILES, 8], f32, m_at + 21568)
        w64 = at("w64", [P, 2, TILES, 64], f32, m_at + 21632)
        rk = at("rk", [P, 8, TILES, NE], f32, m_at + 22656)
        tot = at("tot", [P, 2, NE], f32, m_at + 23168)
        slot = at("slot", [P, 3, TILES, NE], f32, m_at + 23424)
        comb = at("comb", [P, TILES, NE], f32, m_at + 23360)
        plan = at("plan", [P, 2, NE], i32, m_at + 23616)
        planf = at("planf", [P, 4, NE], f32, m_at + 23680)
        glow = at("glow", [HALF, BANK], f32, gains_at + D * 4)
        ulow = at("ulow", [HALF, BANK], f32, gains_at + D * 4 + BANK * 4)

        bank = [ctx.enter_context(nc.psum_tensor(f"bank{i}", [P, BANK], f32)) for i in range(8)]

        def sem(name):
            return ctx.enter_context(nc.semaphore(name))

        arrived = [sem(f"arrived{i}") for i in range(RAW)]
        hi_done = sem("hi_done")
        lo_done = sem("lo_done")
        pe_done = sem("pe_done")
        L = {n: sem(f"ld_{n}") for n in ("x0", "x1", "pos", "gain0", "gain1", "gain2", "gain3", "gain4", "mats",
                                         "freq", "decay", "small", "wdw", "bias1", "bias2", "wr", "route")}
        ss_done = sem("ss_done")
        ms_done = sem("ms_done")
        rstd_done = sem("rstd_done")
        mhalf_set = sem("mhalf_set")
        z_done = sem("z_done")
        zT_done = sem("zT_done")
        xh_done = sem("xh_done")
        xl_done = sem("xl_done")
        ang_done = sem("ang_done")
        trig_done = sem("trig_done")
        acc_free = sem("acc_free")
        half_down = sem("half_down")
        qkT_done = sem("qkT_done")
        qTc = sem("qTc")
        kTc = sem("kTc")
        s_ps = sem("s_ps")
        s_sb = sem("s_sb")
        o_ps = sem("o_ps")
        o_free = sem("o_free")
        gr_var = sem("gr_var")
        gr_rstd = sem("gr_rstd")
        gated = sem("gated")
        oT_ps = sem("oT_ps")
        oTh_done = sem("oTh_done")
        oTl_done = sem("oTl_done")
        res_done = sem("res_done")
        silu_done = sem("silu_done")
        hid_done = sem("hid_done")
        hT_ps = sem("hT_ps")
        hTh_done = sem("hTh_done")
        hTl_done = sem("hTl_done")
        small_ps = sem("small_ps")
        small_sb = sem("small_sb")
        a_gate = sem("a_gate")
        sig_done = sem("sig_done")
        u_done = sem("u_done")
        diag_done = sem("diag_done")
        tap_done = sem("tap_done")
        tap_seq = sem("tap_seq")
        y_pe = sem("y_pe")
        uT_ps = sem("uT_ps")
        uT_sb = sem("uT_sb")
        pad_set = sem("pad_set")
        y_done = sem("y_done")
        mu_ps = sem("mu_ps")
        yc_done = sem("yc_done")
        sq_done = sem("sq_done")
        var_ps = sem("var_ps")
        var_sb = sem("var_sb")
        lnr_done = sem("lnr_done")
        lnd_done = sem("lnd_done")
        lnb_ps = sem("lnb_ps")
        yn_done = sem("yn_done")
        vh_done = sem("vh_done")
        vl_done = sem("vl_done")
        zh_done = sem("zh_done")
        zl_done = sem("zl_done")
        hT32_done = sem("hT32_done")
        hT32b_done = sem("hT32b_done")
        lg_ps = sem("lg_ps")
        lg_max = sem("lg_max")
        ex_done = sem("ex_done")
        sel_done = sem("sel_done")
        rank_ps = sem("rank_ps")
        plan_done = sem("plan_done")
        low_out = sem("low_out")
        folded = sem("folded")
        onehot_done = sem("onehot_done")
        gather_ps = sem("gather_ps")
        xeh_done = sem("xeh_done")
        xel_done = sem("xel_done")
        ohT_ps = sem("ohT_ps")
        ohT_done = sem("ohT_done")
        yh_done = sem("yh_done")
        yl_done = sem("yl_done")
        scat_ps = sem("scat_ps")
        dve_seq = sem("dve_seq")
        act_seq = sem("act_seq")
        out_done = sem("out_done")

        QKT = [6, 7, 0, 1, 2, 3, 4, 5]
        OB = [0, 2, 0, 0]
        DOWN_R = [[bank[2], bank[3]], [bank[4], bank[5]]]
        DOWN = [[bank[4], bank[5]], [bank[6], bank[7]]]
        PE_TAPS = [(c, k) for c in range(DC) for k in range(VECTOR_TAPS.get(c, 0), TAPS)]
        PE_FIRST = TAPS - VECTOR_TAPS[3]

        def taps_to(chunk):
            return sum(c <= chunk for c, k in PE_TAPS)

        SCAT = bank[4:8]

        def by_need(eng, need, piece):
            with eng.If(need > 0):
                with eng.If(need > 1):
                    piece(TWO)
                with eng.Else():
                    piece(PACKED)
            with eng.Else():
                piece(ONE)

        def gather_banks(half, tiles):
            return bank[6:8] if half and tiles == ONE else bank[0:2]

        def need_of(eng, e):
            return eng.value_load(plan[0:1, 0, bass.ds(e, 1)], min_val=0, max_val=2)

        def packed_before(eng, e):
            return eng.value_load(plan[0:1, 1, bass.ds(e, 1)], min_val=0, max_val=STEPS * NE)

        block = ctx.enter_context(nc.Block())

        @block.sync
        def _(sp):
            for t in range(TILES):
                sp.dma_start(res[:, t, :], x[0, t * P:(t + 1) * P, :]).then_inc(L[f"x{t}"], 16)
            sp.dma_start(gains[:, 0, :], norm_mix_g[0].partition_broadcast(P)).then_inc(L["gain0"], 16)

            def load(base, src, six=0):
                if base >= RAW:
                    sp.wait_ge(lo_done, base - RAW + 1 + 6 * six)
                dst = raw[base % RAW][:, :].rearrange("p (c n) -> p c n", c=src.shape[1])
                sp.dma_start(dst, src).then_inc(arrived[base % RAW], 16)

            def cols(w, half, col):
                return w[half * 512:(half + 1) * 512, bass.ds(col, BANK)].rearrange("(c p) n -> p c n", p=P)

            def rows(w, row):
                return w[bass.ds(row, 256), :].rearrange("(c p) n -> p c n", p=P)

            for n in range(12):
                for half in range(2):
                    load(2 * n + half, cols(ret_w_in[0], half, n * BANK))
                if n == 0:
                    sp.dma_start(posi[:, :], positions[0].rearrange("(t p) -> p t", p=P)).then_inc(L["pos"], 16)
                    sp.dma_start(freq[:, :], c_freq.partition_broadcast(P)).then_inc(L["freq"], 16)
                    for i, w in enumerate((conv_b_dw, conv_ln_g, conv_ln_b)):
                        sp.dma_start(small[i * DC:(i + 1) * DC, :], w[0].rearrange("(c p) -> c p", p=P)).then_inc(L["small"], 16)
                    sp.dma_start(wdw[:, :, :], conv_w_dw[0].rearrange("k (c p) -> (k c) p", p=P)
                                 .rearrange("(a r) p -> r a p", a=2)).then_inc(L["wdw"], 16)
            for r in range(8):
                load(B_OUT + r, rows(ret_w_out[0], r * 256))

            def gu(w, base, s, six=0, up_base=None):
                for half in range(2):
                    load(base + half, cols(w, half, s * BANK), six)
                if up_base is None:
                    up(w, base + 2, s, six)

            def up(w, base, s, six=0):
                for half in range(2):
                    load(base + half, cols(w, half, s * BANK + FF), six)

            def down(w, base, s, six=0):
                for r in range(2):
                    load(base + r, rows(w, s * BANK + r * 256), six)

            gu(ffn_w_gu[0], B_FFN, 0)
            with sp.Fori(0, STEPS - 1) as i:
                gu(ffn_w_gu[0], B_FFN + 4, i + 1, i)
                down(ffn_w_down[0], B_FFN + 8, i, i)
            down(ffn_w_down[0], B_PW1 - 2, STEPS - 1)
            for n in range(4):
                for half in range(2):
                    load(B_PW1 + 2 * n + half, cols(conv_w_pw1[0], half, (n // 2 + 2 * (n % 2)) * BANK))
            for r in range(4):
                load(B_PW2 + r, rows(conv_w_pw2[0], r * 256))

            def expert(w, e):
                return w[0, bass.ds(e, 1), :, :].rearrange("a k n -> (a k) n")

            gu(expert(moe_w_gu, 0), B_MOE, 0)

            def steps(cur, j):
                wg, wd = expert(moe_w_gu, cur), expert(moe_w_down, cur)
                with sp.Fori(0, STEPS - 1) as i:
                    gu(wg, B_MOE + 4, i + 1, STEPS * j + i)
                    down(wd, B_MOE + 8, i, STEPS * j + i)

            def seam(cur, nxt, j):
                six = STEPS * j + STEPS - 1
                gu(expert(moe_w_gu, nxt), B_MOE + 4, 0, six, up_base=True)
                down(expert(moe_w_down, cur), B_MOE + 6, STEPS - 1, six)
                up(expert(moe_w_gu, nxt), B_MOE + 8, 0, six)

            with sp.Fori(0, NE - 1) as e:
                steps(e, e)
                seam(e, e + 1, e)
            steps(NE - 1, NE - 1)
            down(expert(moe_w_down, NE - 1), B_MOE + 4, STEPS - 1, STEPS * NE - 1)

            for t in range(TILES):
                for h in range(2):
                    sp.wait_ge(z_done, 16 + 2 * t + h + 1)
                    cols = slice(h * BANK, (h + 1) * BANK)
                    sp.dma_start(out[0, t * P:(t + 1) * P, cols], z[:, t, cols]).then_inc(out_done, 16)
            sp.wait_ge(out_done, 64)

        @block.gpsimd
        def _(pool):
            nc.gpsimd.memset(mhalf[:, :], -0.5).then_inc(mhalf_set, 1)
            nc.gpsimd.memset(ss[:, :], 0.0).then_inc(mhalf_set, 1)
            pool.wait_ge(mhalf_set, 2)

            def root(k):
                for t in range(TILES):
                    pool.wait_ge(ms_done, 2 * k + t + 1)
                    nc.gpsimd.tensor_tensor(rstd[:, t:t + 1], ms[:, t:t + 1], mhalf[:, 0:1], ALU.pow).then_inc(rstd_done, 1)

            root(0)
            for h in range(HEADS):
                pool.wait_ge(gr_var, h + 1)
                nc.gpsimd.tensor_tensor(gr[:, 1, 2 * h:2 * h + 2], gr[:, 0, 2 * h:2 * h + 2], mhalf[:, 0:2],
                                        ALU.pow).then_inc(gr_rstd, 1)
            root(1)
            root(2)
            nc.gpsimd.memset(uT[:, :, 0:PAD], 0.0).then_inc(pad_set, 1)
            pool.wait_ge(var_sb, 1)
            nc.gpsimd.tensor_tensor(lnv[:, 1, :], lnv[:, 0, :], mhalf[:, 0:2], ALU.pow).then_inc(lnr_done, 1)
            root(3)
            root(4)

        @block.scalar
        def _(act):
            seq = [0]

            def own(ins):
                seq[0] += 1
                ins.then_inc(act_seq, 1)
                act.wait_ge(act_seq, seq[0])

            act.dma_start(mats[:, :, :], c_mats).then_inc(L["mats"], 16)

            def squares(k):
                for t in range(TILES):
                    if k == 0:
                        act.wait_ge(L[f"x{t}"], 16)
                        act.wait_ge(mhalf_set, 2)
                    else:
                        act.wait_ge(res_done, 2 * (k - 1 if k < 4 else k - 2 + NE) + t + 1)
                    nc.scalar.activation(z[:, t, :], res[:, t, :], ACT.Square, accum_out=ss[:, t:t + 1]).then_inc(ss_done, 1)

            def hi(base, six=0):
                act.wait_ge(arrived[base % RAW], 16 * (base // RAW + 1) + 16 * six)
                if base >= SPLIT:
                    act.wait_ge(pe_done, base - SPLIT + 1 + 6 * six)
                nc.scalar.activation(whi[base % SPLIT][:, :], raw[base % RAW][:, :], ACT.Copy).then_inc(hi_done, 1)

            def xh_evac(k):
                for t in range(TILES):
                    for q in range(2):
                        act.wait_ge(zT_done, 4 * k + 2 * t + q + 1)
                        nc.scalar.activation(xh[:, 4 * q:4 * q + 4, t * P:(t + 1) * P],
                                             bank[2 * t + q][:, :].rearrange("p (c n) -> p c n", c=4),
                                             ACT.Copy).then_inc(xh_done, 1)

            squares(0)
            hi(0)
            xh_evac(0)
            act.dma_start(gains[:, 1, :], norm_ffn_g[0].partition_broadcast(P)).then_inc(L["gain1"], 16)
            act.dma_start(decay[:, :, :], c_decay).then_inc(L["decay"], 16)
            hi(1)

            def vg(n):
                act.wait_ge(pe_done, 2 * n + 2)
                if n == 4:
                    act.wait_ge(acc_free, 4)
                for t in range(TILES):
                    dst = (v if n < 8 else sg)[:, n % 4, t, :]
                    last = nc.scalar.activation(dst, bank[2 * (n % 3) + t][:, :], ACT.Copy if n < 8 else ACT.Silu)
                last.then_inc(acc_free, 1)

            for n in range(1, 12):
                hi(2 * n)
                hi(2 * n + 1)
                if n == 1:
                    act.wait_ge(small_ps, 1)
                    nc.scalar.activation(smallT[:, :], bank[4][:, 256:280], ACT.Copy).then_inc(small_sb, 1)
                    nc.scalar.activation(wdwT[:, :], bank[4][:, 0:248], ACT.Copy).then_inc(small_sb, 1)
                    act.wait_ge(ang_done, 1)
                    nc.scalar.activation(cs[:, 0, :, :], ang[:, 1, :, :], ACT.Sin).then_inc(trig_done, 1)
                    nc.scalar.activation(cs[:, 1, :, :], ang[:, 0, :, :], ACT.Sin).then_inc(trig_done, 1)
                if n - 2 >= 4:
                    vg(n - 2)
            vg(10)
            hi(B_OUT)
            vg(11)
            for h in range(HEADS):
                act.wait_ge(qkT_done, 2 * h + 1)
                nc.scalar.activation(qT[:, 2 * h:2 * h + 2, :], bank[QKT[2 * h]][:, :].rearrange("p (c n) -> p c n", c=2),
                                     ACT.Copy).then_inc(qTc, 1)

            def gate(h):
                for t in range(TILES):
                    act.wait_ge(o_free, 2 * h + t + 1)
                    act.wait_ge(gr_rstd, h + 1)
                    nc.scalar.activation(o[:, h, t, :], o[:, h, t, :], ACT.Copy,
                                         scale=gr[:, 1, 2 * h + t:2 * h + t + 1]).then_inc(gated, 1)

            def oTh_evac(h):
                for t in range(TILES):
                    act.wait_ge(oT_ps, 2 * h + t + 1)
                    nc.scalar.activation(oTh[:, 4 * h:4 * h + 4, t * P:(t + 1) * P],
                                         bank[6 + t][:, :].rearrange("p (c n) -> p c n", c=4), ACT.Copy).then_inc(oTh_done, 1)

            hi(B_OUT + 1)
            gate(0)
            gate(1)
            oTh_evac(0)
            hi(B_OUT + 2)
            gate(2)
            hi(B_OUT + 3)
            oTh_evac(1)
            hi(B_OUT + 4)
            gate(3)
            hi(B_OUT + 5)
            oTh_evac(2)
            hi(B_OUT + 6)
            hi(B_OUT + 7)
            oTh_evac(3)
            act.wait_ge(z_done, 4)
            act.dma_start(gains[:, 0, :], norm_mix_g[1].partition_broadcast(P)).then_inc(L["gain2"], 16)
            hi(B_FFN)
            squares(1)
            hi(B_FFN + 1)
            xh_evac(1)
            act.dma_start(gains[:, 1, :], norm_ffn_g[1].partition_broadcast(P)).then_inc(L["gain3"], 16)

            def silu(s, before, tiles, n=None):
                act.wait_ge(pe_done, before)
                if s is not None:
                    act.wait_ge(hid_done, s)
                last = nc.scalar.activation(sgate[:, 0, :], bank[0][:, :], ACT.Silu)
                if tiles == TWO:
                    last = nc.scalar.activation(sgate[:, 1, :], bank[1][:, :], ACT.Silu)
                elif tiles == PACKED:
                    act.wait_ge(folded, 2 * n + 1)
                    last = nc.scalar.activation(sgate[0:HALF, 1, :], glow[:, :], ACT.Silu)
                last.then_inc(silu_done, 1)

            def low(dst, src, used, tiles):
                if tiles == PACKED:
                    act.wait_ge(pe_done, used)
                    nc.scalar.activation(dst[:, :], src[HALF:P, :], ACT.Copy).then_inc(low_out, 1)

            def hTh_evac(s, tiles):
                act.wait_ge(hT_ps, s)
                last = nc.scalar.activation(hTh[:, :, 0:P], bank[2][:, :].rearrange("p (c n) -> p c n", c=4), ACT.Copy)
                if tiles == TWO:
                    last = nc.scalar.activation(hTh[:, :, P:SEQ], bank[3][:, :].rearrange("p (c n) -> p c n", c=4),
                                                ACT.Copy)
                elif tiles == PACKED:
                    last = nc.scalar.activation(hTh[:, :, P:P + HALF],
                                                bank[3][:, 0:SEQ].rearrange("p (c n) -> p c n", c=4), ACT.Copy)
                last.then_inc(hTh_done, 1)

            def step(base, s, tiles, six=0, then=None, n=None, ahead=False):
                if not ahead:
                    hi(base, six)
                    hi(base + 1, six)
                hTh_evac(s, tiles)
                hi(base + 2, six)
                hi(base + 3, six)
                low(glow, bank[1], base + 2 + 6 * six, tiles)
                hi(base + 4, six)
                silu(s, base + 2 + 6 * six, tiles, n)
                hi(base + 5, six)
                if then is not None:
                    then()
                low(ulow, bank[3], base + 4 + 6 * six, tiles)

            hi(B_FFN + 2)
            hi(B_FFN + 3)
            hi(B_FFN + 4)
            silu(None, B_FFN + 2, TILES)
            hi(B_FFN + 5)
            hTh_evac(1, TILES)
            hi(B_FFN + 6)
            hi(B_FFN + 7)
            hi(B_FFN + 8)
            silu(1, B_FFN + 6, TILES)
            hi(B_FFN + 9)
            with act.Fori(0, STEPS - 2) as i:
                step(B_FFN + 10, i + 2, TILES, i)
            hi(B_PW1 - 2)
            hTh_evac(STEPS, TILES)
            hi(B_PW1 - 1)

            act.dma_start(bias1[:, :], conv_b_pw1[0].partition_broadcast(P)).then_inc(L["bias1"], 16)
            act.dma_start(bias2[:, :], conv_b_pw2[0].partition_broadcast(P)).then_inc(L["bias2"], 16)
            hi(B_PW1)
            squares(2)
            hi(B_PW1 + 1)
            xh_evac(2)
            act.dma_start(wr[:, :, :], moe_w_router[0].rearrange("(c p) e -> p c e", p=P)).then_inc(L["wr"], 16)
            act.dma_start(route[:, :], c_route.partition_broadcast(P)).then_inc(L["route"], 16)
            act.wait_ge(z_done, 12)
            act.dma_start(gains[:, 0, :], final_norm_g.partition_broadcast(P)).then_inc(L["gain4"], 16)
            for b in range(2, 5):
                hi(B_PW1 + b)

            def glu_evac(half):
                for t in range(TILES):
                    act.wait_ge(a_gate, 2 * half + t + 1)
                    nc.scalar.activation(ug[:, t, half * BANK:(half + 1) * BANK], ug[:, t, half * BANK:(half + 1) * BANK],
                                         ACT.Sigmoid).then_inc(sig_done, 1)

            def uT_evac(half):
                for t in range(TILES):
                    act.wait_ge(uT_ps, 2 * half + t + 1)
                    nc.scalar.activation(uT[:, 4 * half:4 * half + 4, PAD + t * P:PAD + (t + 1) * P],
                                         bank[4 * half + t][:, :].rearrange("p (c n) -> p c n", c=4),
                                         ACT.Copy).then_inc(uT_sb, 1)

            glu_evac(0)
            hi(B_PW1 + 5)
            hi(B_PW1 + 6)
            uT_evac(0)
            hi(B_PW1 + 7)

            def build(m):
                c, k = PE_TAPS[m]
                if m >= 8:
                    act.wait_ge(tap_done, m - 7)
                nc.scalar.activation(diag[:, m % 8, :], ident, ACT.Copy,
                                     scale=wdwT[:, k * DC + c:k * DC + c + 1]).then_inc(diag_done, 1)

            for m in range(8):
                build(m)
            glu_evac(1)
            for m in range(8, PE_FIRST + 8):
                build(m)
            uT_evac(1)
            for m in range(PE_FIRST + 8, len(PE_TAPS)):
                build(m)
                if (m - PE_FIRST) % 14 == 0 and (m - PE_FIRST) // 14 <= 3:
                    hi(B_PW2 + (m - PE_FIRST) // 14 - 1)
                c, k = PE_TAPS[m]
                if k == 3 and c >= 6:
                    act.wait_ge(tap_done, taps_to(c - 1))
                    nc.scalar.activation(y[:, c - 1, :], bank[c - 1][:, 0:SEQ], ACT.Identity,
                                         bias=smallT[:, c - 1:c]).then_inc(y_pe, 1)
            act.wait_ge(tap_done, len(PE_TAPS))
            nc.scalar.activation(y[:, 7, :], bank[7][:, 0:SEQ], ACT.Identity, bias=smallT[:, 7:8]).then_inc(y_pe, 1)
            for c in range(DC):
                act.wait_ge(yc_done, c + 1)
                nc.scalar.activation(sq[:, c, :], y[:, c, :], ACT.Square).then_inc(sq_done, 1)
            for t in range(TILES):
                act.wait_ge(lnr_done, 1)
                nc.scalar.activation(diag[:, t, :], ident, ACT.Copy, scale=lnv[:, 1, t:t + 1]).then_inc(lnd_done, 1)
            for c in range(DC):
                act.wait_ge(yn_done, c + 1)
                own(nc.scalar.activation(y[:, c, :], y[:, c, :], ACT.Silu, bias=smallT[:, 2 * DC + c:2 * DC + c + 1],
                                         scale=smallT[:, DC + c:DC + c + 1]))
                nc.scalar.activation(xh[:, c, :], y[:, c, :], ACT.Copy).then_inc(vh_done, 1)
            hi(B_PW2 + 3)
            hi(B_MOE)

            squares(3)
            hi(B_MOE + 1)
            for t in range(TILES):
                act.wait_ge(zT_done, 12 + 2 * t + 1)
                nc.scalar.activation(hT32[:, 0:4, t * P:(t + 1) * P],
                                     bank[2 * t][:, :].rearrange("p (c n) -> p c n", c=4), ACT.Copy).then_inc(hT32_done, 1)
            for t in range(TILES):
                act.wait_ge(z_done, 12 + 2 * t + 2)
                nc.scalar.activation(zh[:, t, :], z[:, t, :], ACT.Copy).then_inc(zh_done, 1)
            nc.scalar.activation(identr[:, :], ident, ACT.Copy).then_inc(zh_done, 1)
            act.wait_ge(lg_max, 1)
            nc.scalar.activation(rk[:, 0, :, :], rk[:, 7, :, :], ACT.Exp).then_inc(ex_done, 1)

            def xeh_evac(e, half, tiles=TWO):
                act.wait_ge(gather_ps, 2 * e + half + 1)
                for q in range(2):
                    last = nc.scalar.activation(xh[:, 4 * half + 2 * q:4 * half + 2 * q + 2, :],
                                                gather_banks(half, tiles)[q][:, :].rearrange("p (c n) -> p c n", c=2),
                                                ACT.Copy)
                last.then_inc(xeh_done, 1)

            def ohT_evac(e):
                act.wait_ge(ohT_ps, e + 1)
                nc.scalar.activation(onehotT[:, :, :], bank[0][:, :].rearrange("p (s n) -> p s n", s=2),
                                     ACT.Copy).then_inc(ohT_done, 1)

            def y_hi(used, tiles):
                act.wait_ge(pe_done, used)
                for s in range(min(tiles, 2)):
                    for n in range(2):
                        last = nc.scalar.activation(yh[:, s, n * BANK:(n + 1) * BANK], DOWN[s][n][:, :], ACT.Copy)
                last.then_inc(yh_done, 1)

            def expert_steps(e, need, last=False):
                s0, six0, n = STEPS * e + (STEPS + 1), STEPS * e, packed_before(act, e)

                def piece(tiles):
                    step(B_MOE + 4, s0, tiles, six0, lambda: ohT_evac(e), n + 1, ahead=True)
                    with act.Fori(0, STEPS - 3) as i:
                        step(B_MOE + 10, s0 + 1 + i, tiles, six0 + i, n=n + 2 + i)
                    step(B_MOE + 34, s0 + 5, tiles, six0, None if last else lambda: xeh_evac(e + 1, 0), n + 6)

                by_need(act, need, piece)

            hi(B_MOE + 2)
            xeh_evac(0, 0)
            xeh_evac(0, 1, ONE)
            hi(B_MOE + 3)
            act.wait_ge(plan_done, 1)

            def first_gates(tiles):
                low(glow, bank[1], B_MOE + 2, tiles)
                silu(STEPS, B_MOE + 2, tiles, 0)
                low(ulow, bank[3], B_MOE + 4, tiles)

            by_need(act, need_of(act, 0), first_gates)

            hi(B_MOE + 4)
            hi(B_MOE + 5)
            with act.Fori(0, NE - 1) as e:
                need, need_next = need_of(act, e), need_of(act, e + 1)
                expert_steps(e, need)
                s, six = STEPS * e + 2 * STEPS, STEPS * e + (STEPS - 1)
                hi(B_MOE + 4, six)
                by_need(act, need, lambda tiles: xeh_evac(e + 1, 1, tiles))
                hi(B_MOE + 5, six)
                by_need(act, need, lambda tiles: hTh_evac(s, tiles))
                hi(B_MOE + 6, six)
                hi(B_MOE + 7, six)
                n = packed_before(act, e + 1)

                def next_gates(tiles):
                    low(glow, bank[1], B_MOE + 6 + 6 * six, tiles)
                    hi(B_MOE + 8, six)
                    silu(s, B_MOE + 6 + 6 * six, tiles, n)
                    hi(B_MOE + 9, six)

                by_need(act, need_next, next_gates)
                by_need(act, need, lambda tiles: y_hi(B_MOE + 8 + 6 * six, tiles))
                hi(B_MOE + 10, six)
                hi(B_MOE + 11, six)
                with act.If(need_next == 1):
                    low(ulow, bank[3], B_MOE + 10 + 6 * six, PACKED)
            need = need_of(act, NE - 1)
            expert_steps(NE - 1, need, last=True)
            six = STEPS * NE - 1
            hi(B_MOE + 4, six)
            by_need(act, need, lambda tiles: hTh_evac(STEPS * NE + STEPS, tiles))
            hi(B_MOE + 5, six)
            by_need(act, need, lambda tiles: y_hi(B_MOE + 6 + 6 * six, tiles))
            squares(4)

        @block.vector
        def _(dve):
            seq = [0]

            def own(ins):
                seq[0] += 1
                ins.then_inc(dve_seq, 1)
                dve.wait_ge(dve_seq, seq[0])

            def lo(base, six=0):
                dve.wait_ge(hi_done, base + 1 + 6 * six)
                nc.vector.tensor_tensor(wlo[base % SPLIT][:, :], raw[base % RAW][:, :],
                                        whi[base % SPLIT][:, :].bitcast(f32), ALU.subtract).then_inc(lo_done, 1)

            def mean_square(k, t):
                dve.wait_ge(ss_done, 2 * k + t + 1)
                nc.vector.tensor_scalar(ms[:, t:t + 1], ss[:, t:t + 1], 1.0 / D, EPS, ALU.mult, ALU.add).then_inc(ms_done, 1)

            def normalise(k, t):
                dve.wait_ge(L[f"gain{k}"], 16)
                dve.wait_ge(rstd_done, 2 * k + t + 1)
                for h in range(2):
                    cols = slice(h * BANK, (h + 1) * BANK)
                    nc.vector.scalar_tensor_tensor(z[:, t, cols], res[:, t, cols], rstd[:, t:t + 1],
                                                   gains[:, k % 2, cols], ALU.mult, ALU.mult).then_inc(z_done, 1)

            def norm(k):
                for t in range(TILES):
                    mean_square(k, t)
                    normalise(k, t)

            def xl_evac(k):
                for t in range(TILES):
                    for q in range(2):
                        dve.wait_ge(xh_done, 4 * k + 2 * t + q + 1)
                        nc.vector.tensor_tensor(xl[:, 4 * q:4 * q + 4, t * P:(t + 1) * P],
                                                bank[2 * t + q][:, :].rearrange("p (c n) -> p c n", c=4),
                                                xh[:, 4 * q:4 * q + 4, t * P:(t + 1) * P].bitcast(f32),
                                                ALU.subtract).then_inc(xl_done, 1)

            norm(0)
            lo(0)
            xl_evac(0)
            lo(1)
            dve.wait_ge(L["pos"], 16)
            dve.wait_ge(L["freq"], 16)
            own(nc.vector.tensor_copy(posf[:, :], posi[:, :]))
            for t in range(TILES):
                last = nc.vector.tensor_scalar(ang[:, 0, t, :], freq[:, :], posf[:, t:t + 1], None, ALU.mult)
            own(last)
            MAGIC = 12582912.0
            own(nc.vector.tensor_scalar(ang[:, 1, :, :], ang[:, 0, :, :], 1.0 / (2 * np.pi), MAGIC, ALU.mult, ALU.add))
            own(nc.vector.tensor_scalar(ang[:, 1, :, :], ang[:, 1, :, :], -MAGIC, None, ALU.add))
            c1 = 6.28125
            c2 = float(np.float32(int((2 * np.pi - c1) * 2 ** 21) / 2 ** 21))
            c3 = float(2 * np.pi - c1 - c2)
            for c in (c1, c2, c3):
                own(nc.vector.scalar_tensor_tensor(ang[:, 0, :, :], ang[:, 1, :, :], -c, ang[:, 0, :, :],
                                                   ALU.mult, ALU.add))
            PI = 3.1415925
            own(nc.vector.tensor_scalar(ang[:, 0, :, :], ang[:, 0, :, :], PI, -PI, ALU.min, ALU.max))
            own(nc.vector.tensor_scalar(ang[:, 2, :, :], ang[:, 0, :, :], -1.0, None, ALU.mult))
            own(nc.vector.tensor_tensor(ang[:, 2, :, :], ang[:, 2, :, :], ang[:, 0, :, :], ALU.max))
            nc.vector.tensor_scalar(ang[:, 1, :, :], ang[:, 2, :, :], -1.0, float(np.pi / 2), ALU.mult,
                                    ALU.add).then_inc(ang_done, 1)

            def rope(n):
                dve.wait_ge(pe_done, 2 * n + 2)
                if n == 0:
                    dve.wait_ge(trig_done, 2)
                for t in range(TILES):
                    src = bank[2 * (n % 3) + t][:, :].rearrange("p (a d) -> p a d", a=4)
                    a = tmp[:, 0, :].rearrange("p (a d) -> p a d", a=4)
                    b = tmp[:, 1, :].rearrange("p (a d) -> p a d", a=4)
                    cos = cs[:, 0, t, :].unsqueeze(1).to_broadcast([P, 4, P])
                    sin = cs[:, 1, t, :].unsqueeze(1).to_broadcast([P, 4, P])
                    dst = qk[:, n // 2, t, (n % 2) * BANK:(n % 2 + 1) * BANK].rearrange("p (h a d) -> p h a d", h=2, a=2)
                    ah = tmp[:, 0, :].rearrange("p (h a d) -> p h a d", h=2, a=2)
                    bh = tmp[:, 1, :].rearrange("p (h a d) -> p h a d", h=2, a=2)
                    nc.vector.tensor_tensor(a, src, cos, ALU.mult)
                    own(nc.vector.tensor_tensor(b, src, sin, ALU.mult))
                    nc.vector.tensor_tensor(dst[:, :, 0, :], ah[:, :, 0, :], bh[:, :, 1, :], ALU.subtract)
                    last = nc.vector.tensor_tensor(dst[:, :, 1, :], ah[:, :, 1, :], bh[:, :, 0, :], ALU.add)
                    if t == 0:
                        own(last)
                last.then_inc(acc_free, 1)
                dve.wait_ge(acc_free, n + 1)

            for n in range(1, 12):
                lo(2 * n)
                lo(2 * n + 1)
                if 0 <= n - 2 < 4:
                    rope(n - 2)
            lo(B_OUT)
            for h in range(HEADS):
                dve.wait_ge(qkT_done, 2 * h + 2)
                nc.vector.tensor_copy(kT[:, 2 * h:2 * h + 2, :],
                                      bank[QKT[2 * h + 1]][:, :].rearrange("p (c n) -> p c n", c=2)).then_inc(kTc, 1)
            dve.wait_ge(L["decay"], 16)

            def decayed(h):
                dve.wait_ge(s_ps, h + 1)
                if h >= 2:
                    dve.wait_ge(o_ps, 2 * (h - 2) + 2)
                nc.vector.tensor_tensor(S[:, h % 2, :], bank[6 + h % 2][:, 0:384], decay[:, h, :], ALU.mult).then_inc(s_sb, 1)

            def head(h):
                for t in range(TILES):
                    m = 2 * h + t
                    ob = bank[OB[h] + t][:, :]
                    dve.wait_ge(o_ps, m + 1)
                    own(nc.vector.bn_stats(stat[:, m, :], ob))
                    own(nc.vector.bn_aggr(mv[:, m, :], stat[:, m, :]))
                    if t == TILES - 1:
                        nc.vector.tensor_scalar(gr[:, 0, 2 * h:2 * h + 2], mv[:, 2 * h:2 * h + 2, 1], EPS, None,
                                                ALU.add).then_inc(gr_var, 1)
                for t in range(TILES):
                    m = 2 * h + t
                    nc.vector.scalar_tensor_tensor(o[:, h, t, :], bank[OB[h] + t][:, :], mv[:, m, 0:1], sg[:, h, t, :],
                                                   ALU.subtract, ALU.mult).then_inc(o_free, 1)

            def oTl_evac(h):
                for t in range(TILES):
                    dve.wait_ge(oTh_done, 2 * h + t + 1)
                    nc.vector.tensor_tensor(oTl[:, 4 * h:4 * h + 4, t * P:(t + 1) * P],
                                            bank[6 + t][:, :].rearrange("p (c n) -> p c n", c=4),
                                            oTh[:, 4 * h:4 * h + 4, t * P:(t + 1) * P].bitcast(f32),
                                            ALU.subtract).then_inc(oTl_done, 1)

            decayed(0)
            decayed(1)
            head(0)
            decayed(2)
            head(1)
            decayed(3)
            lo(B_OUT + 1)
            oTl_evac(0)
            head(2)
            lo(B_OUT + 2)
            lo(B_OUT + 3)
            oTl_evac(1)
            lo(B_OUT + 4)
            head(3)
            lo(B_OUT + 5)
            oTl_evac(2)
            lo(B_OUT + 6)
            lo(B_OUT + 7)
            oTl_evac(3)

            def residual(n, used, banks=DOWN):
                for t in range(TILES):
                    if t == 0:
                        dve.wait_ge(half_down, n)
                    else:
                        dve.wait_ge(pe_done, used)
                    for h in range(2):
                        cols = slice(h * BANK, (h + 1) * BANK)
                        last = nc.vector.tensor_tensor(res[:, t, cols], banks[t][h][:, :], res[:, t, cols], ALU.add)
                    last.then_inc(res_done, 1)
                    if t == 0:
                        mean_square(n, 0)
                normalise(n, 0)
                mean_square(n, 1)
                normalise(n, 1)

            lo(B_FFN)
            residual(1, B_FFN, DOWN_R)
            xl_evac(1)
            lo(B_FFN + 1)

            def fold(low, src, count):
                dve.wait_ge(low_out, count)
                nc.vector.tensor_tensor(low[:, :], src[0:HALF, :], low[:, :], ALU.add).then_inc(folded, 1)

            def hidden(s, used, tiles, n=None):
                dve.wait_ge(pe_done, used)
                dve.wait_ge(silu_done, s + 1)
                last = nc.vector.tensor_tensor(hid[:, 0, :], bank[2][:, :], sgate[:, 0, :], ALU.mult)
                if tiles == TWO:
                    last = nc.vector.tensor_tensor(hid[:, 1, :], bank[3][:, :], sgate[:, 1, :], ALU.mult)
                elif tiles == PACKED:
                    fold(ulow, bank[3], 2 * n + 2)
                    dve.wait_ge(folded, 2 * n + 2)
                    last = nc.vector.tensor_tensor(hid[0:HALF, 1, :], ulow[:, :], sgate[0:HALF, 1, :], ALU.mult)
                last.then_inc(hid_done, 1)

            def hTl_evac(s, tiles):
                dve.wait_ge(hTh_done, s)
                last = nc.vector.tensor_tensor(hTl[:, :, 0:P], bank[2][:, :].rearrange("p (c n) -> p c n", c=4),
                                               hTh[:, :, 0:P].bitcast(f32), ALU.subtract)
                if tiles == TWO:
                    last = nc.vector.tensor_tensor(hTl[:, :, P:SEQ], bank[3][:, :].rearrange("p (c n) -> p c n", c=4),
                                                   hTh[:, :, P:SEQ].bitcast(f32), ALU.subtract)
                elif tiles == PACKED:
                    last = nc.vector.tensor_tensor(hTh[:, :, P + HALF:SEQ],
                                                   bank[3][:, 0:SEQ].rearrange("p (c n) -> p c n", c=4),
                                                   hTh[:, :, P:P + HALF].bitcast(f32), ALU.subtract)
                last.then_inc(hTl_done, 1)

            def step(base, s, tiles, six=0, then=None, ahead=False, n=None):
                if not ahead:
                    lo(base, six)
                    lo(base + 1, six)
                hTl_evac(s, tiles)
                for b in range(2, 6):
                    lo(base + b, six)
                    if b == 3 and tiles == PACKED:
                        fold(glow, bank[1], 2 * n + 1)
                if then is not None:
                    then()
                hidden(s, base + 4 + 6 * six, tiles, n)

            def vl(c):
                dve.wait_ge(vh_done, c + 1)
                nc.vector.tensor_tensor(xl[:, c, :], y[:, c, :], xh[:, c, :].bitcast(f32), ALU.subtract).then_inc(vl_done, 1)

            for b in range(2, 6):
                lo(B_FFN + b)
                if b == 4:
                    hidden(0, B_FFN + 4, TILES)
            hTl_evac(1, TILES)
            for b in range(6, 10):
                lo(B_FFN + b)
            hidden(1, B_FFN + 8, TILES)
            with dve.Fori(0, STEPS - 2) as i:
                step(B_FFN + 10, i + 2, TILES, i)
            lo(B_PW1 - 2)
            hTl_evac(STEPS, TILES)
            lo(B_PW1 - 1)
            lo(B_PW1)
            residual(2, B_PW1)
            xl_evac(2)
            for b in range(1, 5):
                lo(B_PW1 + b)
            dve.wait_ge(L["bias1"], 16)

            def glu(half):
                cols, gcols = slice(half * BANK, (half + 1) * BANK), slice(D + half * BANK, D + (half + 1) * BANK)
                dve.wait_ge(pe_done, B_PW1 + 4 * half + 4)
                for t in range(TILES):
                    nc.vector.tensor_tensor(ug[:, t, cols], bank[4 * half + 2 + t][:, :], bias1[:, gcols],
                                            ALU.add).then_inc(a_gate, 1)
                for t in range(TILES):
                    last = nc.vector.tensor_tensor(ua[:, t, cols], bank[4 * half + t][:, :], bias1[:, cols], ALU.add)
                own(last)
                for t in range(TILES):
                    dve.wait_ge(sig_done, 2 * half + t + 1)
                    nc.vector.tensor_tensor(ua[:, t, cols], ua[:, t, cols], ug[:, t, cols], ALU.mult).then_inc(u_done, 1)

            glu(0)
            for b in range(5, 8):
                lo(B_PW1 + b)
            dve.wait_ge(small_sb, 2)
            dve.wait_ge(pad_set, 1)
            dve.wait_ge(uT_sb, 2)
            done = {c: 0 for c in range(5)}
            count = [0]

            def tap(c, k):
                if k:
                    dve.wait_ge(tap_seq, done[c])
                w = wdwT[:, k * DC + c:k * DC + c + 1]
                if k == 0:
                    ins = nc.vector.tensor_scalar(y[:, c, :], uT[:, c, 0:SEQ], w, smallT[:, c:c + 1], ALU.mult, ALU.add)
                else:
                    ins = nc.vector.scalar_tensor_tensor(y[:, c, :], uT[:, c, k:k + SEQ], w, y[:, c, :], ALU.mult, ALU.add)
                ins.then_inc(tap_seq, 1)
                count[0] += 1
                done[c] = count[0]

            for k in range(EARLY_TAPS):
                for c in range(4):
                    tap(c, k)
            glu(1)
            for k in range(EARLY_TAPS, TAPS):
                if k == EARLY_TAPS + 2:
                    dve.wait_ge(uT_sb, 4)
                if k - EARLY_TAPS in (5, 10, 15):
                    lo(B_PW2 + (k - EARLY_TAPS) // 5 - 1)
                for c in range(4):
                    if k < VECTOR_TAPS[c]:
                        tap(c, k)
                if 0 <= k - EARLY_TAPS - 2 < VECTOR_TAPS[4]:
                    tap(4, k - EARLY_TAPS - 2)
            dve.wait_ge(tap_seq, count[0])
            dve.wait_ge(tap_done, taps_to(4))
            for c in (3, 4):
                last = nc.vector.tensor_tensor(y[:, c, :], bank[c][:, 0:SEQ], y[:, c, :], ALU.add)
            last.then_inc(y_done, 1)
            dve.wait_ge(mu_ps, 1)
            own(nc.vector.tensor_scalar(mean[:, :], bank[0][:, 0:SEQ], 1.0 / D, None, ALU.mult))
            for c in range(DC):
                nc.vector.tensor_tensor(y[:, c, :], y[:, c, :], mean[:, :], ALU.subtract).then_inc(yc_done, 1)
            dve.wait_ge(var_ps, 1)
            own(nc.vector.tensor_tensor(diag[:, 2:4, :], bank[1][:, 0:SEQ].rearrange("p (t n) -> p t n", t=TILES),
                                        ident.unsqueeze(1).to_broadcast([P, TILES, P]), ALU.mult))
            own(nc.vector.reduce_sum(lnv[:, 1, :], diag[:, 2:4, :], AX.X))
            nc.vector.tensor_scalar(lnv[:, 0, :], lnv[:, 1, :], 1.0 / D, EPS, ALU.mult, ALU.add).then_inc(var_sb, 1)
            dve.wait_ge(lnb_ps, 1)
            for c in range(DC):
                nc.vector.tensor_tensor(y[:, c, :], y[:, c, :], bank[2][:, 0:SEQ], ALU.mult).then_inc(yn_done, 1)
                if c >= 2:
                    vl(c - 2)
            for c in range(DC - 2, DC):
                vl(c)
            lo(B_PW2 + 3)
            dve.wait_ge(L["bias2"], 16)
            for t in range(TILES):
                last = nc.vector.tensor_tensor(res[:, t, :], res[:, t, :], bias2[:, :], ALU.add)
            own(last)
            lo(B_MOE)
            residual(3, B_MOE)
            for t in range(TILES):
                dve.wait_ge(zT_done, 12 + 2 * t + 2)
                nc.vector.tensor_copy(hT32[:, 4:8, t * P:(t + 1) * P],
                                      bank[2 * t + 1][:, :].rearrange("p (c n) -> p c n", c=4)).then_inc(hT32b_done, 1)
            lo(B_MOE + 1)
            dve.wait_ge(L["route"], 16)
            dve.wait_ge(lg_ps, 1)
            own(nc.vector.tensor_copy(lg[:, :, :], bank[4][:, 0:TILES * NE].rearrange("p (t e) -> p t e", t=TILES)))
            before = route[:, :].rearrange("p (a b) -> p a b", a=NE)
            for t in range(TILES):
                le = lg[:, t, :].unsqueeze(2).to_broadcast([P, NE, NE])
                lf = lg[:, t, :].unsqueeze(1).to_broadcast([P, NE, NE])
                nc.vector.tensor_tensor(w64[:, 0, t, :].rearrange("p (a b) -> p a b", a=NE), lf, le, ALU.is_gt)
                last = nc.vector.tensor_tensor(w64[:, 1, t, :].rearrange("p (a b) -> p a b", a=NE), lf, le, ALU.is_equal)
            own(last)
            own(nc.vector.tensor_tensor(w64[:, 1, :, :], w64[:, 1, :, :],
                                        route[:, :].unsqueeze(1).to_broadcast([P, TILES, 64]), ALU.mult))
            own(nc.vector.tensor_tensor(w64[:, 0, :, :], w64[:, 0, :, :], w64[:, 1, :, :], ALU.add))
            own(nc.vector.reduce_sum(rk[:, 1, :, :], w64[:, 0, :, :].rearrange("p t (a b) -> p t a b", a=NE), AX.X))
            own(nc.vector.tensor_scalar(rk[:, 2, :, :], rk[:, 1, :, :], 1.5, None, ALU.is_lt))
            nc.vector.tensor_copy(rk[:, 4, :, :], rk[:, 2, :, :]).then_inc(sel_done, 1)
            for t in range(TILES):
                own(nc.vector.max(srt[:, t, :], lg[:, t, :]))
                last = nc.vector.tensor_scalar(rk[:, 7, t, :], lg[:, t, :], srt[:, t, 0:1], None, ALU.subtract)
            last.then_inc(lg_max, 1)
            for t in range(TILES):
                dve.wait_ge(zh_done, t + 1)
                nc.vector.tensor_tensor(zl[:, t, :], z[:, t, :], zh[:, t, :].bitcast(f32), ALU.subtract).then_inc(zl_done, 1)
            dve.wait_ge(rank_ps, 1)
            pref = bank[5][:, 0:TILES * NE].rearrange("p (t e) -> p t e", t=TILES)
            own(nc.vector.scalar_tensor_tensor(rk[:, 5, :, :], pref, 1.0, rk[:, 2, :, :], ALU.add, ALU.mult))
            for i in range(2):
                nc.vector.tensor_scalar(planf[:, i, :], bank[5][:, 2 * NE:3 * NE], P + i * HALF + 0.5, None, ALU.is_gt)
            for s in range(2):
                last = nc.vector.tensor_scalar(slot[:, s, :, :], rk[:, 5, :, :], -1.0 - s * P, None, ALU.add)
            own(last)
            own(nc.vector.tensor_tensor(planf[:, 2, :], planf[:, 0, :], planf[:, 1, :], ALU.subtract))
            own(nc.vector.scalar_tensor_tensor(slot[:, 2, :, :], planf[:, 2, :].unsqueeze(1).to_broadcast([P, TILES, NE]),
                                               float(HALF), slot[:, 1, :, :], ALU.mult, ALU.add))

            def build_onehot(e):
                for i, (a, b) in enumerate(((0, P), (0, HALF), (HALF, P))):
                    at_ = (0, P, P)[i]
                    for t in range(TILES):
                        last = nc.vector.tensor_scalar(onehot[:, t, at_ + a:at_ + b], iota[:, a:b],
                                                       slot[:, i, t, bass.ds(e, 1)], None, ALU.is_equal)
                last.then_inc(onehot_done, 1)

            build_onehot(0)
            ahead = w64[:, 0, 0, :].rearrange("p (a b) -> p a b", a=NE)
            own(nc.vector.scalar_tensor_tensor(ahead, planf[:, 2, :].unsqueeze(1).to_broadcast([P, NE, NE]), float(STEPS),
                                               before, ALU.mult, ALU.mult))
            own(nc.vector.reduce_sum(planf[:, 3, :], ahead, AX.X))
            nc.vector.tensor_copy(plan[:, 1, :], planf[:, 3, :])
            nc.vector.tensor_tensor(plan[:, 0, :], planf[:, 0, :], planf[:, 1, :], ALU.add).then_inc(plan_done, 1)

            def xel_evac(e, half, need, banks):
                def piece(tiles):
                    dve.wait_ge(xeh_done, 2 * e + half + 1)
                    width = SEQ if tiles == TWO else P
                    for q in range(2):
                        chunks = slice(4 * half + 2 * q, 4 * half + 2 * q + 2)
                        src = banks[q][:, :].rearrange("p (c n) -> p c n", c=2)
                        if tiles == PACKED:
                            nc.vector.tensor_tensor(xh[:, chunks, P + HALF:SEQ], src[:, :, P + HALF:SEQ],
                                                    xh[:, chunks, P:P + HALF].bitcast(f32), ALU.subtract)
                        last = nc.vector.tensor_tensor(xl[:, chunks, 0:width], src[:, :, 0:width],
                                                       xh[:, chunks, 0:width].bitcast(f32), ALU.subtract)
                    last.then_inc(xel_done, 1)

                by_need(dve, need, piece)

            lo(B_MOE + 2)
            dve.wait_ge(plan_done, 1)
            need = need_of(dve, 0)
            dve.wait_ge(ex_done, 1)
            own(nc.vector.tensor_tensor(rk[:, 3, :, :], rk[:, 0, :, :], rk[:, 2, :, :], ALU.mult))
            own(nc.vector.reduce_sum(tot[:, 0, 0:TILES], rk[:, 3, :, :], AX.X))
            xel_evac(0, 0, need, gather_banks(0, ONE))
            own(nc.vector.reciprocal(tot[:, 0, 2:2 + TILES], tot[:, 0, 0:TILES]))
            for t in range(TILES):
                last = nc.vector.tensor_scalar(comb[:, t, :], rk[:, 3, t, :], tot[:, 0, 2 + t:3 + t], None, ALU.mult)
            own(last)
            xel_evac(0, 1, need, gather_banks(1, ONE))
            lo(B_MOE + 3)

            def first_hidden(tiles):
                if tiles == PACKED:
                    fold(glow, bank[1], 1)
                hidden(STEPS, B_MOE + 4, tiles, 0)

            by_need(dve, need, first_hidden)

            def y_lo(e, need):
                def piece(tiles):
                    dve.wait_ge(yh_done, e + 1)
                    for s in range(min(tiles, 2)):
                        for n in range(2):
                            cols = slice(n * BANK, (n + 1) * BANK)
                            last = nc.vector.tensor_tensor(yl[:, s, cols], DOWN[s][n][:, :], yh[:, s, cols].bitcast(f32),
                                                           ALU.subtract)
                    last.then_inc(yl_done, 1)

                by_need(dve, need, piece)

            def accumulate(e):
                dve.wait_ge(scat_ps, e + 1)
                for t in range(TILES):
                    for n in range(2):
                        cols = slice(n * BANK, (n + 1) * BANK)
                        last = nc.vector.scalar_tensor_tensor(res[:, t, cols], SCAT[2 * t + n][:, :],
                                                              comb[:, t, bass.ds(e, 1)], res[:, t, cols],
                                                              ALU.mult, ALU.add)
                    last.then_inc(res_done, 1)

            def next_onehot(e):
                dve.wait_ge(ohT_ps, e + 1)
                build_onehot(e + 1)

            def expert_steps(e, need, need_next=None):
                s0, six0, n = STEPS * e + (STEPS + 1), STEPS * e, packed_before(dve, e)

                def piece(tiles):
                    step(B_MOE + 4, s0, tiles, six0, lambda: next_onehot(e) if need_next is not None else None,
                         ahead=True, n=n + 1)
                    with dve.Fori(0, STEPS - 3) as i:
                        step(B_MOE + 10, s0 + 1 + i, tiles, six0 + i, n=n + 2 + i)
                    step(B_MOE + 34, s0 + 5, tiles, six0,
                         lambda: xel_evac(e + 1, 0, need_next, bank[0:2]) if need_next is not None else None, n=n + 6)

                by_need(dve, need, piece)

            lo(B_MOE + 4)
            lo(B_MOE + 5)
            with dve.Fori(0, NE - 1) as e:
                need, need_next = need_of(dve, e), need_of(dve, e + 1)
                expert_steps(e, need, need_next)
                s, six = STEPS * e + 2 * STEPS, STEPS * e + (STEPS - 1)
                lo(B_MOE + 4, six)
                by_need(dve, need, lambda tiles: xel_evac(e + 1, 1, need_next, gather_banks(1, tiles)))
                lo(B_MOE + 5, six)
                by_need(dve, need, lambda tiles: hTl_evac(s, tiles))
                lo(B_MOE + 6, six)
                lo(B_MOE + 7, six)
                n = packed_before(dve, e + 1)
                with dve.If(need_next == 1):
                    fold(glow, bank[1], 2 * n + 1)
                lo(B_MOE + 8, six)
                lo(B_MOE + 9, six)
                y_lo(e, need)
                by_need(dve, need_next, lambda tiles: hidden(s, B_MOE + 10 + 6 * six, tiles, n))
                lo(B_MOE + 10, six)
                lo(B_MOE + 11, six)
                accumulate(e)
            need = need_of(dve, NE - 1)
            expert_steps(NE - 1, need)
            six = STEPS * NE - 1
            lo(B_MOE + 4, six)
            by_need(dve, need, lambda tiles: hTl_evac(STEPS * NE + STEPS, tiles))
            lo(B_MOE + 5, six)
            y_lo(NE - 1, need)
            accumulate(NE - 1)
            norm(4)

        @block.tensor
        def _(pe):
            def product(dst, ah, al, bh, bl, start, stop):
                nc.tensor.matmul(dst, ah, bh, start=start, stop=False)
                last = nc.tensor.matmul(dst, ah, bl, start=False, stop=stop and al is None)
                if al is None:
                    return last
                return nc.tensor.matmul(dst, al, bh, start=False, stop=stop)

            def columns(base, acc, half, ready=None, tiles=TILES, six=0):
                pe.wait_ge(lo_done, base + 1 + 6 * six)
                slot_ = base % SPLIT
                for t in range(min(tiles, 2)):
                    if ready is not None:
                        pe.wait_ge(xl_done, ready + 2 * t + 2)
                    for c in range(4):
                        kc = 4 * half + c
                        tok = slice(t * P, (t + 1) * P)
                        last = product(acc[t][:, :], xh[:, kc, tok], None if t and tiles == PACKED else xl[:, kc, tok],
                                       whi[slot_][:, c * BANK:(c + 1) * BANK], wlo[slot_][:, c * BANK:(c + 1) * BANK],
                                       kc == 0, kc == DC - 1)
                last.then_inc(pe_done, 1)

            def rows(base, ah, al, first_chunk, start, stop, tiles=TILES, six=0, banks=DOWN, halves=True):
                pe.wait_ge(lo_done, base + 1 + 6 * six)
                slot_ = base % SPLIT
                for t in range(min(tiles, 2)):
                    for c in range(2):
                        kc = first_chunk + c
                        tok = slice(t * P, (t + 1) * P)
                        for n in range(2):
                            col = c * D + n * BANK
                            last = product(banks[t][n][:, :], ah[:, kc, tok],
                                           None if t and tiles == PACKED else al[:, kc, tok],
                                           whi[slot_][:, col:col + BANK], wlo[slot_][:, col:col + BANK],
                                           start and c == 0, stop and c == 1)
                    if stop and t == 0 and halves:
                        last.then_inc(half_down, 1)
                last.then_inc(pe_done, 1)

            def turn(k):
                for t in range(TILES):
                    for c in range(DC):
                        if c % 4 == 0:
                            pe.wait_ge(z_done, 4 * k + 2 * t + c // 4 + 1)
                        last = nc.tensor.transpose(bank[2 * t + c // 4][:, c % 4 * P:(c % 4 + 1) * P],
                                                   z[:, t, c * P:(c + 1) * P], ident)
                        if c % 4 == 3:
                            last.then_inc(zT_done, 1)

            pe.wait_ge(L["mats"], 16)
            turn(0)
            for n in range(3):
                if n == 2:
                    pe.wait_ge(small_sb, 2)
                for half in range(2):
                    columns(2 * n + half, bank[2 * n:2 * n + 2], half, 0 if n == 0 else None)
                if n == 0:
                    pe.wait_ge(L["wdw"], 16)
                    pe.wait_ge(L["small"], 48)
                    for a in range(2):
                        nc.tensor.transpose(bank[4][:, a * 124:(a + 1) * 124], wdw[:, a, :], ident[0:124, 0:124])
                    nc.tensor.transpose(bank[4][:, 256:280], small[:, :], ident[0:24, 0:24]).then_inc(small_ps, 1)
            with pe.Fori(0, 3) as i:
                for n in range(3):
                    pe.wait_ge(acc_free, 3 * i + n + 1)
                    for half in range(2):
                        columns(6 + 2 * n + half, bank[2 * n:2 * n + 2], half, six=i)
            for m in range(8):
                h = m // 2
                pe.wait_ge(acc_free, (4, 4, 10, 10, 11, 11, 12, 12)[m])
                for cc in range(2):
                    c = 2 * h + cc
                    for t in range(TILES):
                        last = nc.tensor.transpose(bank[QKT[m]][:, cc * SEQ + t * P:cc * SEQ + (t + 1) * P],
                                                   qk[:, m % 2, t, c * P:(c + 1) * P], ident)
                last.then_inc(qkT_done, 1)

            def scores(h):
                pe.wait_ge(qTc, h + 1)
                pe.wait_ge(kTc, h + 1)
                if h >= 2:
                    pe.wait_ge(s_sb, h - 1)
                dst = bank[6 + h % 2]
                for dc in range(2):
                    nc.tensor.matmul(dst[:, 0:SEQ], kT[:, 2 * h + dc, 0:P], qT[:, 2 * h + dc, :],
                                     start=dc == 0, stop=dc == 1)
                for dc in range(2):
                    last = nc.tensor.matmul(dst[:, SEQ:384], kT[:, 2 * h + dc, P:SEQ], qT[:, 2 * h + dc, P:SEQ],
                                            start=dc == 0, stop=dc == 1)
                last.then_inc(s_ps, 1)

            def values(h):
                pe.wait_ge(s_sb, h + 1)
                if h == 0:
                    pe.wait_ge(qTc, 2)
                    pe.wait_ge(kTc, 2)
                elif h == 1:
                    pe.wait_ge(qTc, 3)
                    pe.wait_ge(kTc, 3)
                elif h == 2:
                    pe.wait_ge(o_free, 2)
                else:
                    pe.wait_ge(o_free, 6)
                dst = bank[OB[h]]
                nc.tensor.matmul(dst[:, :], S[:, h % 2, 0:P], v[:, h, 0, :], start=True, stop=True).then_inc(o_ps, 1)
                dst = bank[OB[h] + 1]
                nc.tensor.matmul(dst[:, :], S[:, h % 2, P:SEQ], v[:, h, 0, :], start=True, stop=False)
                nc.tensor.matmul(dst[:, :], S[:, h % 2, SEQ:384], v[:, h, 1, :], start=False, stop=True).then_inc(o_ps, 1)

            def o_turn(h):
                pe.wait_ge(s_sb, 4)
                if h:
                    pe.wait_ge(oTl_done, 2 * h)
                for t in range(TILES):
                    pe.wait_ge(gated, 2 * h + t + 1)
                    for c in range(4):
                        last = nc.tensor.transpose(bank[6 + t][:, c * P:(c + 1) * P], o[:, h, t, c * P:(c + 1) * P], ident)
                    last.then_inc(oT_ps, 1)

            def project(r):
                pe.wait_ge(oTl_done, 2 * (r // 2) + 2)
                if r == 0:
                    pe.wait_ge(o_free, 4)
                    pe.wait_ge(kTc, 4)
                    pe.wait_ge(qTc, 4)
                rows(B_OUT + r, oTh, oTl, 2 * r, r == 0, r == 7, banks=DOWN_R)

            scores(0)
            scores(1)
            values(0)
            scores(2)
            values(1)
            scores(3)
            o_turn(0)
            values(2)
            project(0)
            o_turn(1)
            project(1)
            values(3)
            project(2)
            o_turn(2)
            project(3)
            project(4)
            o_turn(3)
            for r in range(5, 8):
                project(r)

            def hT_turn(s, tiles, shared=None):
                pe.wait_ge(hid_done, s + 1)
                for t in range(min(tiles, 2)):
                    rows_ = HALF if t and tiles == PACKED else P
                    for c in range(4):
                        if shared is not None and t == 0 and c == 3:
                            pe.wait_ge(xel_done, shared)
                        last = nc.tensor.transpose(bank[2 + t][:, c * rows_:(c + 1) * rows_],
                                                   hid[0:rows_, t, c * P:(c + 1) * P], ident[0:rows_, 0:rows_])
                last.then_inc(hT_ps, 1)

            def step(base, s, tiles, first=False, six=0, between=None, then=None, shared=None):
                pe.wait_ge(silu_done, s)
                columns(base, bank[0:2], 0, tiles=tiles, six=six)
                columns(base + 1, bank[0:2], 1, tiles=tiles, six=six)
                pe.wait_ge(hTl_done, s)
                columns(base + 2, bank[2:4], 0, tiles=tiles, six=six)
                columns(base + 3, bank[2:4], 1, tiles=tiles, six=six)
                if between is not None:
                    pe.wait_ge(silu_done, s + 1)
                    between()
                rows(base + 4, hTh, hTl, 0, first, False, tiles, six)
                rows(base + 5, hTh, hTl, 2, False, False, tiles, six)
                if then is not None:
                    then()
                hT_turn(s, tiles, shared)

            turn(1)
            pe.wait_ge(xl_done, 6)
            for half in range(2):
                columns(B_FFN + half, bank[0:2], half, 4)
            for half in range(2):
                columns(B_FFN + 2 + half, bank[2:4], half)
            hT_turn(0, TILES)
            pe.wait_ge(res_done, 2)
            step(B_FFN + 4, 1, TILES, True)
            with pe.Fori(0, STEPS - 2) as i:
                step(B_FFN + 10, i + 2, TILES, six=i)
            pe.wait_ge(hTl_done, STEPS)
            rows(B_PW1 - 2, hTh, hTl, 0, False, False)
            rows(B_PW1 - 1, hTh, hTl, 2, False, True)

            turn(2)
            pe.wait_ge(xl_done, 10)

            def u_turn(half):
                for t in range(TILES):
                    pe.wait_ge(u_done, 2 * half + t + 1)
                    for c in range(4):
                        col = half * BANK + c * P
                        last = nc.tensor.transpose(bank[4 * half + t][:, c * P:(c + 1) * P], ua[:, t, col:col + P], ident)
                    last.then_inc(uT_ps, 1)

            for b in range(8):
                n = b // 2
                columns(B_PW1 + b, bank[2 * n:2 * n + 2], b % 2, 8 if n == 0 else None)
                if b == 4:
                    u_turn(0)
            pe.wait_ge(uT_sb, 2)
            pe.wait_ge(pad_set, 1)
            for m, (c, k) in enumerate(PE_TAPS):
                if m == PE_FIRST:
                    u_turn(1)
                    pe.wait_ge(uT_sb, 4)
                pe.wait_ge(diag_done, m + 1)
                last = nc.tensor.matmul(bank[c][:, 0:SEQ], diag[:, m % 8, :], uT[:, c, k:k + SEQ],
                                        start=k == VECTOR_TAPS.get(c, 0), stop=k == TAPS - 1)
                last.then_inc(tap_done, 1)
            for n, c in enumerate((5, 6, 0, 1, 2, 3, 4, 7)):
                if c >= 5:
                    pe.wait_ge(y_pe, c - 4)
                else:
                    pe.wait_ge(y_done, 1)
                last = nc.tensor.matmul(bank[0][:, 0:SEQ], ones, y[:, c, :], start=n == 0, stop=n == DC - 1)
            last.then_inc(mu_ps, 1)
            for c in range(DC):
                pe.wait_ge(sq_done, c + 1)
                last = nc.tensor.matmul(bank[1][:, 0:SEQ], ones, sq[:, c, :], start=c == 0, stop=c == DC - 1)
            last.then_inc(var_ps, 1)
            for t in range(TILES):
                pe.wait_ge(lnd_done, t + 1)
                last = nc.tensor.matmul(bank[2][:, t * P:(t + 1) * P], ones, diag[:, t, :], start=True, stop=True)
            last.then_inc(lnb_ps, 1)
            for r in range(4):
                pe.wait_ge(vl_done, 2 * r + 2)
                rows(B_PW2 + r, xh, xl, 2 * r, r == 0, r == 3)

            turn(3)
            pe.wait_ge(res_done, 6)
            pe.wait_ge(L["wr"], 16)
            for t in range(TILES):
                pe.wait_ge(hT32_done, t + 1)
                pe.wait_ge(hT32b_done, t + 1)
                for c in range(DC):
                    last = nc.tensor.matmul(bank[4][:, t * NE:(t + 1) * NE], hT32[:, c, t * P:(t + 1) * P], wr[:, c, :],
                                            start=c == 0, stop=c == DC - 1)
            last.then_inc(lg_ps, 1)
            pe.wait_ge(sel_done, 1)
            nc.tensor.matmul(bank[5][:, 0:NE], earlier, rk[:, 4, 0, :], start=True, stop=True)
            nc.tensor.matmul(bank[5][:, NE:2 * NE], earlier, rk[:, 4, 1, :], start=True, stop=False)
            nc.tensor.matmul(bank[5][:, NE:2 * NE], ones, rk[:, 4, 0, :], start=False, stop=True)
            nc.tensor.matmul(bank[5][:, 2 * NE:3 * NE], ones, rk[:, 4, 0, :], start=True, stop=False)
            nc.tensor.matmul(bank[5][:, 2 * NE:3 * NE], ones, rk[:, 4, 1, :], start=False, stop=True).then_inc(rank_ps, 1)

            def gather(e, half, tiles=TWO):
                pe.wait_ge(onehot_done, e + 1)
                if half and tiles != ONE:
                    pe.wait_ge(xel_done, 2 * e + 1)
                for c in range(4):
                    dst = gather_banks(half, tiles)[c // 2][:, c % 2 * SEQ:(c % 2 + 1) * SEQ]
                    col = half * BANK + c * P
                    for t in range(TILES):
                        nc.tensor.matmul(dst, zh[:, t, col:col + P], onehot[:, t, :], start=t == 0, stop=False)
                        last = nc.tensor.matmul(dst, zl[:, t, col:col + P], onehot[:, t, :], start=False,
                                                stop=t == TILES - 1)
                last.then_inc(gather_ps, 1)

            def onehot_turn(e):
                for s in range(2):
                    for t in range(TILES):
                        last = nc.tensor.matmul(bank[0][:, s * SEQ + t * P:s * SEQ + (t + 1) * P],
                                                onehot[:, t, s * P:(s + 1) * P],
                                                identr[:, :], start=True, stop=True)
                last.then_inc(ohT_ps, 1)
                pe.wait_ge(res_done, 2 * e + 6)

            def scatter(e, need):
                def piece(tiles):
                    pe.wait_ge(yl_done, e + 1)
                    for t in range(TILES):
                        for n in range(2):
                            dst, cols = SCAT[2 * t + n][:, :], slice(n * BANK, (n + 1) * BANK)
                            for s in range(min(tiles, 2)):
                                where = onehotT[:, s, t * P:(t + 1) * P]
                                nc.tensor.matmul(dst, where, yh[:, s, cols], start=s == 0, stop=False)
                                last = nc.tensor.matmul(dst, where, yl[:, s, cols], start=False, stop=s == min(tiles, 2) - 1)
                    last.then_inc(scat_ps, 1)

                by_need(pe, need, piece)

            def gates(base, need, e, s, six=0):
                def piece(half, tiles):
                    pe.wait_ge(silu_done, s)
                    pe.wait_ge(xel_done, 2 * e + half + 1)
                    columns(base + half, bank[0:2], half, tiles=tiles, six=six)

                by_need(pe, need, lambda tiles: piece(0, tiles))
                by_need(pe, need, lambda tiles: piece(1, tiles))

            def ups(base, need, six=0):
                for half in range(2):
                    by_need(pe, need, lambda tiles: columns(base + half, bank[2:4], half, tiles=tiles, six=six))

            def expert_steps(e, need, last=False):
                s0, six0 = STEPS * e + (STEPS + 1), STEPS * e

                def piece(tiles):
                    step(B_MOE + 4, s0, tiles, True, six0, between=lambda: onehot_turn(e),
                         then=lambda: pe.wait_ge(ohT_done, e + 1))
                    with pe.Fori(0, STEPS - 3) as i:
                        step(B_MOE + 10, s0 + 1 + i, tiles, six=six0 + i)
                    if last:
                        step(B_MOE + 34, s0 + 5, tiles, six=six0)
                    elif tiles == ONE:
                        step(B_MOE + 34, s0 + 5, 1, six=six0, between=lambda: (gather(e + 1, 0), gather(e + 1, 1, 1)))
                    else:
                        step(B_MOE + 34, s0 + 5, tiles, six=six0, between=lambda: gather(e + 1, 0),
                             then=lambda: gather(e + 1, 1), shared=2 * e + 4)

                by_need(pe, need, piece)

            def last_rows(base, need, s, six):
                def piece(r, tiles):
                    pe.wait_ge(hTl_done, s)
                    rows(base + r, hTh, hTl, 2 * r, False, r == 1, tiles, six, halves=False)

                by_need(pe, need, lambda tiles: piece(0, tiles))
                by_need(pe, need, lambda tiles: piece(1, tiles))

            pe.wait_ge(zh_done, 3)
            pe.wait_ge(zl_done, 2)
            gather(0, 0)
            gather(0, 1, ONE)
            pe.wait_ge(plan_done, 1)
            need = need_of(pe, 0)
            gates(B_MOE, need, 0, STEPS)
            ups(B_MOE + 2, need)
            by_need(pe, need, lambda tiles: hT_turn(STEPS, tiles))

            with pe.Fori(0, NE - 1) as e:
                need, need_next = need_of(pe, e), need_of(pe, e + 1)
                expert_steps(e, need)
                s, six = STEPS * e + 2 * STEPS, STEPS * e + (STEPS - 1)
                gates(B_MOE + 4, need_next, e + 1, s, six)
                last_rows(B_MOE + 6, need, s, six)
                ups(B_MOE + 8, need_next, six)
                scatter(e, need)
                by_need(pe, need_next, lambda tiles: hT_turn(s, tiles))
            need = need_of(pe, NE - 1)
            expert_steps(NE - 1, need, last=True)
            last_rows(B_MOE + 4, need, STEPS * NE + STEPS, STEPS * NE - 1)
            scatter(NE - 1, need)


def constants():
    f = np.float32
    i = np.arange(P)
    mats = np.zeros((P, 4, P), f)
    mats[:, 0] = np.eye(P)
    mats[:, 1] = i[:, None] < i[None, :]
    mats[:, 2] = 1
    mats[:, 3] = i[None, :]
    half = DQK // 2
    freq = (f(10000.0) ** (-np.arange(half, dtype=f) / f(half))).astype(f)
    lg = np.log1p(-(2.0 ** (-5.0 - np.arange(HEADS, dtype=np.float64))))
    rel = i[None, :] - i[:, None]
    decay = np.zeros((P, HEADS, 3, P), np.float64)
    for h in range(HEADS):
        same = np.where(rel >= 0, np.exp(np.maximum(rel, 0) * lg[h]), 0.0)
        cross = np.exp((i[None, :] + 1 + P - 1 - i[:, None]) * lg[h])
        decay[:, h] = np.stack([same, cross, same], 1) * DQK ** -0.5
    e = np.arange(NE)
    route = (e[None, :] < e[:, None]).reshape(-1).astype(f)
    return {"c_mats": mats, "c_freq": freq, "c_decay": decay.reshape(P, HEADS, 384).astype(f), "c_route": route}


INPUTS = ["x", "positions", "norm_mix_g", "norm_ffn_g", "final_norm_g", "ret_w_in", "ret_w_out", "conv_w_pw1",
          "conv_b_pw1", "conv_w_dw", "conv_b_dw", "conv_ln_g", "conv_ln_b", "conv_w_pw2", "conv_b_pw2", "ffn_w_gu",
          "ffn_w_down", "moe_w_router", "moe_w_gu", "moe_w_down"]


def kernel(**inputs):
    import concourse.bacc as bacc
    from concourse.bass_utils import run_bass_kernel_spmd

    nc = bacc.Bacc("TRN2", target_bir_lowering=False, num_devices=1)
    arrays, args = {}, []
    for name, a in [(n, inputs[n]) for n in INPUTS] + list(constants().items()):
        a = np.ascontiguousarray(a)
        arrays[f"in_{name}"] = a
        args.append(nc.dram_tensor(f"in_{name}", a.shape, mybir.dt.from_np(a.dtype), kind="ExternalInput").ap())
    args.append(nc.dram_tensor("out_h", (1, SEQ, D), mybir.dt.float32, kind="ExternalOutput").ap())
    trunk(nc, *args)
    r = run_bass_kernel_spmd(nc, [arrays], core_ids=[0])
    return r.results[0]["out_h"]
```
